# Optimizing a Trainium2 kernel written in Bass

```python
import math
import jax
import jax.numpy as jnp
from jax import lax
import numpy as np

D_MODEL = 2048
BATCH = 1
SEQ = 1024
DEPTH = 1
DEC_BATCH = 8
DEC_SEQ = 4
PAST_LEN = 8192
PAGE_SIZE = 128

ML_H = 4
ML_W = D_MODEL // 2
ML_DH = ML_W // ML_H
SA_H = 4
SA_W = D_MODEL // 4
SA_DH = SA_W // SA_H
MEM_H = 4
MEM_W = D_MODEL // 4
MEM_DH = MEM_W // MEM_H
MIX_W = ML_W + SA_W + MEM_W
IDX_H = 8
IDX_D = 64
IDX_SCALE = (IDX_H * IDX_D) ** -0.5
TOPK_MAX = 256
N_MEM = 256
CHUNK = 64
Q_BLOCK = 128
ROPE_THETA = 10000.0
EPS = 1e-6
F32 = jnp.float32

IN_SPLITS = (
    ('ml_q', ML_W), ('ml_k', ML_W), ('ml_v', ML_W), ('ml_o', ML_W), ('ml_z', ML_W),
    ('ml_i', ML_H), ('ml_f', ML_H),
    ('sa_q', SA_W), ('sa_k', SA_W), ('sa_v', SA_W), ('sa_z', SA_W),
    ('idx_q', IDX_H * IDX_D), ('idx_k', IDX_D), ('idx_w', IDX_H),
    ('mem_q', MEM_W), ('mem_z', MEM_W),
)
IN_W = sum(w for _, w in IN_SPLITS)

kernel_name = 'hymba_mlstm_dsa_memory_decode_step'

def rmsnorm(x, g):
    xf = x.astype(F32)
    y = xf * lax.rsqrt(jnp.mean(xf * xf, axis=-1, keepdims=True) + EPS)
    return (y * g.astype(F32)).astype(x.dtype)

def rope(x, pos):
    half = x.shape[-1] // 2
    inv = ROPE_THETA ** (-jnp.arange(half, dtype=F32) / half)
    ang = pos.astype(F32)[:, None] * inv[None, :]
    cos = jnp.cos(ang)[None, :, None, :]
    sin = jnp.sin(ang)[None, :, None, :]
    x1 = x[..., :half].astype(F32)
    x2 = x[..., half:].astype(F32)
    return jnp.concatenate([x1 * cos - x2 * sin, x1 * sin + x2 * cos], axis=-1).astype(x.dtype)

def split_proj(h):
    out = {}
    off = 0
    for name, w in IN_SPLITS:
        out[name] = h[..., off:off + w]
        off += w
    return out

def mix_in(x, g_pre, w_in):
    return split_proj(rmsnorm(x, g_pre) @ w_in)

def mix_out(x, a, b, c, w_out, g_post):
    hcat = jnp.concatenate([a, b, c], axis=-1)
    return x + rmsnorm(hcat @ w_out, g_post)

def mlstm_chunkwise(q, k, v, ig, lf, C0, n0, m0):
    B, L, H, D = q.shape
    c = math.gcd(L, CHUNK)
    nc = L // c

    def to_chunks(a):
        a = a.reshape((B, nc, c) + a.shape[2:])
        a = jnp.moveaxis(a, 3, 2)
        return jnp.moveaxis(a, 1, 0)

    causal = jnp.tril(jnp.ones((c, c), dtype=bool))

    def step(carry, xs):
        C, n, m = carry
        qc, kc, vc, igc, lfc = xs
        b = jnp.cumsum(lfc, axis=-1)
        a = jnp.where(causal, b[..., :, None] - b[..., None, :] + igc[..., None, :], -jnp.inf)
        m_t = jnp.maximum(b + m[..., None], jnp.max(a, axis=-1))
        inter = jnp.exp(b + m[..., None] - m_t)
        dmat = jnp.exp(a - m_t[..., None])
        s = jnp.einsum('bhtd,bhsd->bhts', qc, kc) * dmat
        num = jnp.einsum('bhts,bhsv->bhtv', s, vc) + inter[..., None] * jnp.einsum('bhtk,bhkv->bhtv', qc, C)
        qn = jnp.sum(s, axis=-1) + inter * jnp.einsum('bhtk,bhk->bht', qc, n)
        h = num / jnp.maximum(jnp.abs(qn), jnp.exp(-m_t))[..., None]
        m_new = m_t[..., -1]
        w_end = jnp.exp(b[..., -1:] - b + igc - m_new[..., None])
        decay = jnp.exp(b[..., -1] + m - m_new)
        C_new = decay[..., None, None] * C + jnp.einsum('bhs,bhsk,bhsv->bhkv', w_end, kc, vc)
        n_new = decay[..., None] * n + jnp.einsum('bhs,bhsk->bhk', w_end, kc)
        return (C_new, n_new, m_new), h

    xs = (to_chunks(q), to_chunks(k), to_chunks(v), to_chunks(ig), to_chunks(lf))
    (C, n, m), hs = lax.scan(step, (C0, n0, m0), xs)
    h = jnp.swapaxes(jnp.moveaxis(hs, 0, 1), 2, 3).reshape(B, L, H, D)
    return h, C, n, m

def mlstm_branch(p, b_gates, g_head, C0, n0, m0, dtype):
    B, L, _ = p['ml_q'].shape
    shp = (B, L, ML_H, ML_DH)
    q = p['ml_q'].reshape(shp).astype(F32)
    k = p['ml_k'].reshape(shp).astype(F32) * (ML_DH ** -0.5)
    v = p['ml_v'].reshape(shp).astype(F32)
    bg = b_gates.astype(F32)
    ig = p['ml_i'].astype(F32) + bg[:ML_H]
    lf = jax.nn.log_sigmoid(p['ml_f'].astype(F32) + bg[ML_H:])
    h, C, n, m = mlstm_chunkwise(q, k, v, ig, lf, C0.astype(F32), n0.astype(F32), m0.astype(F32))
    h = h * lax.rsqrt(jnp.mean(h * h, axis=-1, keepdims=True) + EPS)
    h = h.reshape(B, L, ML_W) * g_head.astype(F32)
    out = h * jax.nn.sigmoid(p['ml_o'].astype(F32)) * jax.nn.silu(p['ml_z'].astype(F32))
    return out.astype(dtype), C, n, m

def dsa_project(p, pos):
    B, L, _ = p['sa_q'].shape
    shp = (B, L, SA_H, SA_DH)
    q = rope(p['sa_q'].reshape(shp), pos)
    k = rope(p['sa_k'].reshape(shp), pos)
    v = p['sa_v'].reshape(shp)
    qi = rope(p['idx_q'].reshape(B, L, IDX_H, IDX_D), pos)
    ki = rope(p['idx_k'][:, :, None, :], pos)[:, :, 0, :]
    return q, k, v, qi, p['idx_w'], ki

def select_keys(qi, wi, ki, valid, n_sel):
    dots = jnp.einsum('bqhd,bkd->bqhk', qi.astype(F32), ki.astype(F32))
    sc = jnp.einsum('bqh,bqhk->bqk', wi.astype(F32) * IDX_SCALE, jax.nn.relu(dots))
    sc = jnp.where(valid[None], sc, -jnp.inf)
    top, idx = lax.top_k(sc, n_sel)
    return idx, top > -jnp.inf

def attend_selected(q, ks, vs, ok):
    s = jnp.einsum('bqhd,bqnhd->bqhn', q.astype(F32), ks.astype(F32)) * (SA_DH ** -0.5)
    s = jnp.where(ok[:, :, None, :], s, -jnp.inf)
    a = jax.nn.softmax(s, axis=-1)
    return jnp.einsum('bqhn,bqnhd->bqhd', a, vs.astype(F32))

def gather_rows(a, idx):
    return jax.vmap(lambda ab, ib: ab[ib])(a, idx)

def dsa_prompt(p, dtype):
    B, L, _ = p['sa_q'].shape
    pos = jnp.arange(L, dtype=jnp.int32)
    q, k, v, qi, wi, ki = dsa_project(p, pos)
    n_sel = min(TOPK_MAX, L // 4)
    qb = math.gcd(L, Q_BLOCK)

    def block(s0):
        q_b = lax.dynamic_slice_in_dim(q, s0, qb, axis=1)
        qi_b = lax.dynamic_slice_in_dim(qi, s0, qb, axis=1)
        wi_b = lax.dynamic_slice_in_dim(wi, s0, qb, axis=1)
        valid = pos[None, :] <= (s0 + jnp.arange(qb, dtype=jnp.int32))[:, None]
        idx, ok = select_keys(qi_b, wi_b, ki, valid, n_sel)
        return attend_selected(q_b, gather_rows(k, idx), gather_rows(v, idx), ok)

    o = lax.map(block, jnp.arange(0, L, qb, dtype=jnp.int32))
    o = jnp.moveaxis(o, 0, 1).reshape(B, L, SA_W)
    out = o * jax.nn.silu(p['sa_z'].astype(F32))
    return out.astype(dtype), k, v, ki

def dsa_sample(p, cache_k, cache_v, cache_kidx, page_table, dtype):
    Bd, T, _ = p['sa_q'].shape
    P = page_table.shape[1] * PAGE_SIZE
    pos = P + jnp.arange(T, dtype=jnp.int32)
    q, k, v, qi, wi, ki = dsa_project(p, pos)
    ki_past = cache_kidx[page_table].reshape(Bd, P, IDX_D).astype(ki.dtype)
    ki_all = jnp.concatenate([ki_past, ki], axis=1)
    n_sel = min(TOPK_MAX, (P + T) // 4)
    valid = jnp.arange(P + T, dtype=jnp.int32)[None, :] <= pos[:, None]
    idx, ok = select_keys(qi, wi, ki_all, valid, n_sel)
    in_past = (idx < P)[..., None, None]
    pc = jnp.minimum(idx, P - 1)
    phys = jax.vmap(lambda pt, ib: pt[ib])(page_table, pc // PAGE_SIZE)
    slot = pc % PAGE_SIZE
    jn = jnp.clip(idx - P, 0, T - 1)
    ks = jnp.where(in_past, cache_k[phys, slot].astype(k.dtype), gather_rows(k, jn))
    vs = jnp.where(in_past, cache_v[phys, slot].astype(v.dtype), gather_rows(v, jn))
    o = attend_selected(q, ks, vs, ok).reshape(Bd, T, SA_W)
    out = o * jax.nn.silu(p['sa_z'].astype(F32))
    return out.astype(dtype), k, v, ki

def mem_kv(mem, g_mem, w_mem_k, w_mem_v):
    B, M, _ = mem.shape
    mn = rmsnorm(mem, g_mem)
    return (mn @ w_mem_k).reshape(B, M, MEM_H, MEM_DH), (mn @ w_mem_v).reshape(B, M, MEM_H, MEM_DH)

def mem_branch(p, mk, mv, dtype):
    B, L, _ = p['mem_q'].shape
    q = p['mem_q'].reshape(B, L, MEM_H, MEM_DH).astype(F32)
    s = jnp.einsum('blhd,bmhd->bhlm', q, mk.astype(F32)) * (MEM_DH ** -0.5)
    a = jax.nn.softmax(s, axis=-1)
    o = jnp.einsum('bhlm,bmhd->blhd', a, mv.astype(F32)).reshape(B, L, MEM_W)
    return (o * jax.nn.silu(p['mem_z'].astype(F32))).astype(dtype)

def layer(x_p, x_s, st_C, st_n, st_m, c_k, c_v, c_kidx, c_mk, c_mv, page_table, mem_prompt,
          g_pre, w_in, b_gates, g_head, w_mem_k, w_mem_v, g_mem, w_out, g_post):
    B = x_p.shape[0]
    pp = mix_in(x_p, g_pre, w_in)
    C0 = jnp.zeros((B, ML_H, ML_DH, ML_DH), F32)
    n0 = jnp.zeros((B, ML_H, ML_DH), F32)
    m0 = jnp.zeros((B, ML_H), F32)
    a_p, pC, pn, pm = mlstm_branch(pp, b_gates, g_head, C0, n0, m0, x_p.dtype)
    b_p, pk, pv, pki = dsa_prompt(pp, x_p.dtype)
    pmk, pmv = mem_kv(mem_prompt, g_mem, w_mem_k, w_mem_v)
    c_p = mem_branch(pp, pmk, pmv, x_p.dtype)
    y_p = mix_out(x_p, a_p, b_p, c_p, w_out, g_post)
    ps = mix_in(x_s, g_pre, w_in)
    a_s, sC, sn, sm = mlstm_branch(ps, b_gates, g_head, st_C, st_n, st_m, x_s.dtype)
    b_s, sk, sv, ski = dsa_sample(ps, c_k, c_v, c_kidx, page_table, x_s.dtype)
    c_s = mem_branch(ps, c_mk, c_mv, x_s.dtype)
    y_s = mix_out(x_s, a_s, b_s, c_s, w_out, g_post)
    return y_p, y_s, (pC, pn, pm, pk, pv, pki, pmk, pmv, sC, sn, sm, sk, sv, ski)

def setup_inputs(seed: int = 0) -> dict:
    key = jax.random.key(seed)
    ks = jax.random.split(key, 24)
    n_pages = PAST_LEN // PAGE_SIZE
    n_used = DEC_BATCH * n_pages
    n_pool = n_used + (n_used + 3) // 4

    def nrm(k, shape, s=1.0):
        return s * jax.random.normal(k, shape, F32)

    page_table = jax.random.permutation(ks[10], n_pool)[:n_used].reshape(DEC_BATCH, n_pages).astype(jnp.int32)
    b_gates = jnp.concatenate([nrm(ks[14], (DEPTH, ML_H), 0.1), 3.0 + nrm(ks[15], (DEPTH, ML_H), 0.5)], axis=-1)
    return {
        'x_prompt': nrm(ks[0], (BATCH, SEQ, D_MODEL)),
        'x_sample': nrm(ks[1], (DEC_BATCH, DEC_SEQ, D_MODEL)),
        'state_mlstm_C': nrm(ks[2], (DEPTH, DEC_BATCH, ML_H, ML_DH, ML_DH), 0.05),
        'state_mlstm_n': nrm(ks[3], (DEPTH, DEC_BATCH, ML_H, ML_DH), 0.5),
        'state_mlstm_m': nrm(ks[4], (DEPTH, DEC_BATCH, ML_H)),
        'cache_k': nrm(ks[5], (DEPTH, n_pool, PAGE_SIZE, SA_H, SA_DH)),
        'cache_v': nrm(ks[6], (DEPTH, n_pool, PAGE_SIZE, SA_H, SA_DH)),
        'cache_kidx': nrm(ks[7], (DEPTH, n_pool, PAGE_SIZE, IDX_D)),
        'cache_mem_k': nrm(ks[8], (DEPTH, DEC_BATCH, N_MEM, MEM_H, MEM_DH)),
        'cache_mem_v': nrm(ks[9], (DEPTH, DEC_BATCH, N_MEM, MEM_H, MEM_DH)),
        'page_table': page_table,
        'mem_prompt': nrm(ks[11], (BATCH, N_MEM, D_MODEL)),
        'g_pre': 1.0 + nrm(ks[12], (DEPTH, D_MODEL), 0.05),
        'w_in': nrm(ks[13], (DEPTH, D_MODEL, IN_W), D_MODEL ** -0.5),
        'b_gates': b_gates,
        'g_head': 1.0 + nrm(ks[16], (DEPTH, ML_W), 0.05),
        'w_mem_k': nrm(ks[17], (DEPTH, D_MODEL, MEM_W), D_MODEL ** -0.5),
        'w_mem_v': nrm(ks[18], (DEPTH, D_MODEL, MEM_W), D_MODEL ** -0.5),
        'g_mem': 1.0 + nrm(ks[19], (DEPTH, D_MODEL), 0.05),
        'w_out': nrm(ks[20], (DEPTH, MIX_W, D_MODEL), MIX_W ** -0.5),
        'g_post': 1.0 + nrm(ks[21], (DEPTH, D_MODEL), 0.05),
    }

def reference(x_prompt, x_sample, state_mlstm_C, state_mlstm_n, state_mlstm_m, cache_k, cache_v,
              cache_kidx, cache_mem_k, cache_mem_v, page_table, mem_prompt, g_pre, w_in, b_gates,
              g_head, w_mem_k, w_mem_v, g_mem, w_out, g_post):
    xp, xs = x_prompt, x_sample
    per_layer = []
    for l in range(DEPTH):
        xp, xs, new = layer(xp, xs, state_mlstm_C[l], state_mlstm_n[l], state_mlstm_m[l],
                            cache_k[l], cache_v[l], cache_kidx[l], cache_mem_k[l], cache_mem_v[l],
                            page_table, mem_prompt, g_pre[l], w_in[l], b_gates[l], g_head[l],
                            w_mem_k[l], w_mem_v[l], g_mem[l], w_out[l], g_post[l])
        per_layer.append(new)
    (p_C, p_n, p_m, p_k, p_v, p_kidx, p_mem_k, p_mem_v,
     s_C, s_n, s_m, s_k, s_v, s_kidx) = [jnp.stack(a) for a in zip(*per_layer)]
    return (xp, xs, p_C, p_n, p_m, p_k, p_v, p_kidx, p_mem_k, p_mem_v, s_C, s_n, s_m, s_k, s_v, s_kidx)


_drawn_inputs = setup_inputs


def setup_inputs(seed=0):
    import zlib

    import numpy as np

    out = dict(_drawn_inputs(seed))
    spreads = {}
    factors = {}
    for name, (base, spread) in spreads.items():
        noise = np.random.default_rng([zlib.crc32(name.encode()), seed]).standard_normal(out[name].shape)
        drawn = base * np.exp(spread * noise) if base else spread * noise
        out[name] = jnp.asarray(drawn.astype(out[name].dtype))
    for name, factor in factors.items():
        out[name] = (out[name] * factor).astype(out[name].dtype)
    return out
```

```python
import math
from contextlib import ExitStack

import numpy as np

import concourse.bass as bass
from concourse import mybir

F32 = mybir.dt.float32
I32 = mybir.dt.int32
U32 = mybir.dt.uint32
ALU = mybir.AluOpType
ACT = mybir.ActivationFunctionType
AX = mybir.AxisListType.X

P = 128
D = 2048
KT = D // P
SEQ = 1024
DEC_B, DEC_T = 8, 4
NS = DEC_B * DEC_T
TOK = SEQ + NS
QT = SEQ // P
ML_H, ML_D = 4, 256
ML_W = ML_H * ML_D
CHUNK = P
NCH = SEQ // CHUNK
H, DH = 4, 128
HW = H * DH
IDX_H, IDX_D = 8, 64
IDX_SCALE = (IDX_H * IDX_D) ** -0.5
N_MEM = 256
TOPK = 256
PAGE, N_PAGES, N_POOL = 128, 64, 640
PAST = PAGE * N_PAGES
EPS = 1e-6
C_Q, C_K, C_V, C_O, C_Z = (ML_W * j for j in range(5))
C_I = 5 * ML_W
C_F = C_I + ML_H
C_SQ = C_F + ML_H
C_SK, C_SV, C_SZ, C_IQ = (C_SQ + HW * j for j in range(1, 5))
C_IK = C_IQ + IDX_H * IDX_D
C_IW = C_IK + IDX_D
C_MQ = C_IW + IDX_H
C_MZ = C_MQ + HW
IN_W = C_MZ + HW
A_BLOCKS, A_W = 8, (IN_W - C_I) // 8
B_BLOCKS, B_W = C_I // 512, 512
T_Q, T_K, T_MQ, T_IQ, T_IK, T_SLOTS = 0, 4, 8, 12, 16, 17
NEG = -3.0e38
TAKEN = -3.3e38


class Order:

    def __init__(self, eng, sem, passed=None):
        self.passed = passed
        self.eng, self.sem, self.total, self.i, self.per = eng, sem, 0, None, 0

    def __call__(self, ins):
        ins.then_inc(self.sem, 1)
        self.total += 1
        return ins

    def then(self):
        self.eng.wait_ge(self.sem, self.total if self.i is None else self.i * self.per + self.total)

    def then_plain(self):
        self.then()
        self.eng.sem_inc(self.passed, 1)

    def step(self, ins):
        self(ins)
        self.then()

    def loop(self, n, per):
        with self.eng.Fori(0, n) as i:
            begin, self.i, self.per = self.total, i, per
            yield i
            assert self.total - begin == per, (self.total - begin, per)
            self.i = None
        self.total = begin + per * n


class Program:
    def __init__(self, nc, ins, outs):
        self.nc, self.ins, self.outs = nc, ins, outs
        self.outer = ExitStack()
        self.names = 0

    def sem(self, name):
        s = self.stage.enter_context(self.nc.semaphore(name))
        self.in_stage.append(s)
        return s

    def queue_sems(self, name, n):
        return [self.outer.enter_context(self.nc.semaphore(f"{name}{j}")) for j in range(n)]

    def run(self, stage):
        with ExitStack() as self.stage:
            self.in_stage = []
            stage(self)
            with self.nc.Block() as block:

                @block.sync
                def _(sp):
                    for s in self.in_stage:
                        sp.sem_clear(s)

    def sems(self, name, n):
        return [self.sem(f"{name}{j}") for j in range(n)]

    def sb(self, name, shape, dt=F32, at=None):
        return (at or self.outer).enter_context(self.nc.sbuf_tensor(name, shape, dt))

    def ps(self, name, shape, at, dt=F32):
        return at.enter_context(self.nc.psum_tensor(name, shape, dt))

    def scratch(self, name, shape, dt=F32):
        return self.nc.dram_tensor(name, shape, dt, kind="Internal").ap()


def pairs(eng, n, *peeled, order=None, per=0):
    if order is not None:
        for i in order.loop(n // 2, per):
            for u in range(2):
                yield i * 2 + u, u, i, None
    else:
        with eng.Fori(0, n // 2) as i:
            for u in range(2):
                yield i * 2 + u, u, i, None
    for j, what in enumerate(peeled):
        yield n + j, (n + j) % 2, (n + j) // 2, what


def normalise(k):
    nc, ins = k.nc, k.ins
    k.x_loaded, k.xn_free = k.sems("x_loaded", 2), k.sem("xn_free")
    x_free, gains = k.sem("x_free"), k.sem("gains_loaded")
    squares, meaned, rooted = k.sem("squares_summed"), k.sem("mean_ready"), k.sem("rstd_ready")
    normed, turned = k.sem("x_normed"), k.sem("x_turned")
    kept_a, kept_v = k.sem("xT_kept_by_act"), k.sem("xT_kept_by_dve")
    halfset = k.sem("minus_half_set")
    with ExitStack() as st:
        xin = k.sb("xin", [P, 2, D], at=st)
        xn = k.sb("xn", [P, 2, D], at=st)
        junk = k.sb("sqjunk", [P, D], at=st)
        gpre = k.sb("gpre", [P, D], at=st)
        gmem = k.sb("gmem", [P, D], at=st)
        ss = k.sb("ss", [P, 2], at=st)
        ms = k.sb("ms", [P, 2], at=st)
        rstd = k.sb("rstd", [P, 2], at=st)
        turn = [k.ps(f"turn{j}", [P, 4, P], st) for j in range(8)]
        rest = (0, 1, 2)

        def rows(what):
            return NS if what == 2 else P

        def place(n, u, i, what):
            if what is None:
                return lambda a, b: k.xT[:, a:b, bass.ds(i * 2 * P + u * P, P)]
            if what == 2:
                return lambda a, b: k.xT[:, a:b, SEQ:TOK]
            return lambda a, b: k.memT[:, a:b, what * P:(what + 1) * P]

        block = st.enter_context(nc.Block())

        @block.sync
        def _(sp):
            sp.dma_start(k.ident[:], ins["ident"][:, :]).then_inc(gains, 16)
            sp.dma_start(gpre[:], ins["g_pre"][0:1, :].partition_broadcast(P)).then_inc(gains, 16)
            sp.dma_start(gmem[:], ins["g_mem"][0:1, :].partition_broadcast(P)).then_inc(gains, 16)
            for n, u, i, what in pairs(sp, QT, *rest):
                r = rows(what)
                src = {None: None, 0: ins["mem_prompt"][0:P, :], 1: ins["mem_prompt"][P:2 * P, :],
                       2: ins["x_sample"][:, :]}[what]
                if what is None:
                    src = ins["x_prompt"][bass.ds(n * P, P), :]
                sp.wait_ge(x_free, n + 1)
                sp.dma_start(xin[0:r, u, :], src).then_inc(k.x_loaded[u], 16)

        @block.scalar
        def _(act):
            for n, u, i, what in pairs(act, QT, *rest):
                r = rows(what)
                act.wait_ge(k.x_loaded[u], i * 16 + 16)
                act.wait_ge(x_free, n + 1)
                act.wait_ge(squares, n + 1)
                nc.scalar.activation(junk[0:r, :], xin[0:r, u, :], ACT.Square,
                                     accum_out=ss[0:r, u:u + 1]).then_inc(squares, 1)
                act.wait_ge(turned, n + 1)
                put = place(n, u, i, what)
                for b in range(2):
                    nc.scalar.activation(put(4 * b, 4 * b + 4), turn[4 * u + b][:, :, 0:r],
                                         ACT.Copy).then_inc(kept_a, 1)

        @block.gpsimd
        def _(pool):
            nc.gpsimd.memset(k.mhalf[:], -0.5).then_inc(halfset, 1)
            pool.wait_ge(halfset, 1)
            for n, u, i, what in pairs(pool, QT, *rest):
                r = rows(what)
                pool.wait_ge(meaned, n + 1)
                nc.gpsimd.tensor_tensor(rstd[0:r, u:u + 1], ms[0:r, u:u + 1], k.mhalf[0:r, :],
                                        ALU.pow).then_inc(rooted, 1)

        @block.vector
        def _(dve):
            dve.sem_inc(x_free, 2)
            dve.sem_inc(squares, 1)
            dve.wait_ge(gains, 48)
            for n, u, i, what in pairs(dve, QT, *rest):
                r = rows(what)
                g = gpre if what in (None, 2) else gmem
                dve.wait_ge(squares, n + 2)
                nc.vector.tensor_scalar(ms[0:r, u:u + 1], ss[0:r, u:u + 1], 1.0 / D, EPS, ALU.mult,
                                        ALU.add).then_inc(meaned, 1)
                dve.wait_ge(rooted, n + 1)
                dve.wait_ge(k.xn_free, n + 1)
                nc.vector.scalar_tensor_tensor(xn[0:r, u, :], xin[0:r, u, :], rstd[0:r, u:u + 1],
                                               g[0:r, :], ALU.mult, ALU.mult).then_inc(normed, 1)
                dve.wait_ge(normed, n + 1)
                dve.sem_inc(x_free, 1)
                dve.wait_ge(turned, n + 1)
                put = place(n, u, i, what)
                for b in range(2, 4):
                    nc.vector.tensor_copy(put(4 * b, 4 * b + 4),
                                          turn[4 * u + b][:, :, 0:r]).then_inc(kept_v, 1)

        @block.tensor
        def _(pe):
            pe.sem_inc(k.xn_free, 2)
            pe.sem_inc(kept_a, 4)
            pe.sem_inc(kept_v, 4)
            pe.wait_ge(gains, 48)
            for n, u, i, what in pairs(pe, QT, *rest):
                r = rows(what)
                pe.wait_ge(normed, n + 1)
                pe.wait_ge(kept_a, 2 * n + 2)
                pe.wait_ge(kept_v, 2 * n + 2)
                for c in range(KT):
                    last = nc.tensor.transpose(turn[4 * u + c // 4][:, c % 4, 0:r],
                                               xn[0:r, u, c * P:(c + 1) * P], k.ident[0:r, 0:r])
                last.then_inc(turned, 1)
                pe.wait_ge(turned, n + 1)
                pe.sem_inc(k.xn_free, 1)


N_TILES = QT + 1
P_BANKS = 6


class Projection:

    def __init__(self, k, tag, n_blocks, width, col0):
        self.k, self.n, self.w, self.c0 = k, n_blocks, width, col0
        self.between = []
        self.loaded = k.sems(f"w_loaded_{tag}", 2)
        self.free = k.sem(f"w_free_{tag}")
        self.done = k.sem(f"bank_ready_{tag}")
        self.copied = k.sem(f"bank_copied_{tag}")
        self.stored = k.sems(f"stored_{tag}", P_BANKS)

    def rows(self, t):
        return (t * P, P) if t < QT else (SEQ, NS)

    def load(self, sp, b, u):
        sp.wait_ge(self.free, b + 1)
        for part in range(2):
            sp.dma_start(self.k.w[:, u, 8 * part:8 * part + 8, 0:self.w],
                         self.k.w_in_v[:, 8 * part:8 * part + 8, bass.ds(b * self.w + self.c0, self.w)]
                         ).then_inc(self.loaded[u], 16)

    def store(self, sp, b, u, i):
        for t in range(N_TILES):
            r0, r = self.rows(t)
            m = N_TILES * u + t
            sp.wait_ge(self.copied, i * 2 * N_TILES + m + 1 + P_BANKS)
            sp.dma_start(self.k.proj[r0:r0 + r, bass.ds(b * self.w + self.c0, self.w)],
                         self.k.pout[0:r, m % P_BANKS, 0:self.w]).then_inc(self.stored[m % P_BANKS], 16)

    def sync(self, sp, before_last=lambda: None):
        self.load(sp, 0, 0)
        with sp.Fori(0, self.n // 2 - 1) as i:
            for u in range(2):
                self.load(sp, i * 2 + u + 1, 1 - u)
                self.store(sp, i * 2 + u, u, i)
        i = self.n // 2 - 1
        self.load(sp, self.n - 1, 1)
        self.store(sp, self.n - 2, 0, i)
        before_last()
        self.store(sp, self.n - 1, 1, i)
        for j in range(P_BANKS):
            sp.wait_ge(self.stored[j], 16 * (self.n * N_TILES // P_BANKS + 1))

    def scalar(self, act, *segments):
        for j in range(P_BANKS):
            act.sem_inc(self.stored[j], 16)
        act.sem_inc(self.copied, P_BANKS)
        first = 0
        for n, function in segments or ((self.n // 2, ACT.Copy),):
            with act.Fori(first, first + n) as i:
                self.evacuate(act, i, function)
            first += n
            if first < self.n // 2 and self.between:
                self.between.pop(0)()

    def evacuate(self, act, i, function):
        per = 2 * N_TILES
        for m in range(per):
            r = self.rows(m % N_TILES)[1]
            j = m % P_BANKS
            act.wait_ge(self.done, i * per + m + 1)
            act.wait_ge(self.stored[j], (i * (per // P_BANKS) + m // P_BANKS) * 16 + 16)
            self.k.nc.scalar.activation(self.k.pout[0:r, j, 0:self.w], self.k.bank[j][0:r, 0:self.w],
                                        function).then_inc(self.copied, 1)

    def credit(self, pe):
        pe.sem_inc(self.free, 2)

    def tensor(self, pe):
        k = self.k
        per = 2 * N_TILES
        with pe.Fori(0, self.n // 2) as i:
            for u in range(2):
                pe.wait_ge(self.loaded[u], i * 32 + 32)
                for t in range(N_TILES):
                    r0, r = self.rows(t)
                    m = N_TILES * u + t
                    pe.wait_ge(self.copied, i * per + m + 1)
                    for c in range(KT):
                        last = k.nc.tensor.matmul(k.bank[m % P_BANKS][0:r, 0:self.w],
                                                  k.xT[:, c, r0:r0 + r], k.w[:, u, c, 0:self.w],
                                                  start=c == 0, stop=c == KT - 1)
                    last.then_inc(self.done, 1)
                pe.wait_ge(self.done, i * per + N_TILES * (u + 1))
                pe.sem_inc(self.free, 1)


class Gates:

    def __init__(self, k, st):
        S = k.sem
        T = lambda name, shape: k.sb("gate_" + name, shape, F32, at=st)
        self.k = k
        self.loaded, self.steps, self.acted, self.ready, self.order, self.stored = (
            S("gates_loaded"), S("gate_steps"), S("gate_act"), S("gate_rows_ready"), S("gate_order"), S("gates_stored"))
        self.tables = [T(n, [ML_H, TOK]) for n in ("i", "f", "lf", "b", "m", "t", "rst", "isf")]
        self.small = [T("bias", [ML_H, 2])] + [T(n, [ML_H, 16]) for n in ("m0", "mp", "mn", "bl", "dk")]

    def load(self, sp):
        k, ins, g_in = self.k, self.k.ins, self.loaded
        gi, gf, _, _, _, _, rst, isf = self.tables
        bg, m0, *_ = self.small
        for c, dst in ((C_I, gi), (C_F, gf)):
            sp.dma_start(dst[:, :], k.proj[:, c:c + ML_H].rearrange("t h -> h t")).then_inc(g_in, 16)
        sp.dma_start(bg[:, :], ins["b_gates"][0:1, :].rearrange("o (g h) -> (o h) g", g=2)).then_inc(g_in, 16)
        sp.dma_start(m0[:, 0:DEC_B], ins["state_mlstm_m"].rearrange("b h -> h b")).then_inc(g_in, 16)
        sp.dma_start(rst[:, :], ins["not_first"][0:1, :].partition_broadcast(ML_H)).then_inc(g_in, 16)
        sp.dma_start(isf[:, :], ins["dec_first"][0:1, :].partition_broadcast(ML_H)).then_inc(g_in, 16)

    def store(self, sp):
        k, outs = self.k, self.k.outs
        gi, gf, lf, bb, mm, t1, _, _ = self.tables
        dk = self.small[5]
        sp.wait_ge(self.ready, 1)
        for j, x in enumerate((bb, lf, gf, t1, gi)):
            sp.dma_start(k.grows[j, :, :], x[:, :]).then_inc(self.stored, 16)
        sp.dma_start(k.gdecay[:, :], dk[:, :]).then_inc(self.stored, 16)
        sp.dma_start(outs["prompt_m"][:, :], mm[:, SEQ - 1:SEQ]).then_inc(self.stored, 16)
        sp.dma_start(outs["sample_m"].rearrange("b h -> h b"),
                     mm[:, SEQ:TOK].rearrange("p (c t) -> p c t", t=DEC_T)[:, :, DEC_T - 1]).then_inc(self.stored, 16)

    def scalar(self, act):
        nc, g_abs, g_act = self.k.nc, self.steps, self.acted
        gi, _, lf, _, mm, t1, _, _ = self.tables
        dk = self.small[5]
        act.wait_ge(g_abs, 1)
        nc.scalar.activation(t1[:], t1[:], ACT.Exp, scale=-1.0).then_inc(g_act, 1)
        act.wait_ge(g_abs, 2)
        nc.scalar.activation(t1[:], t1[:], ACT.Ln).then_inc(g_act, 1)
        act.wait_ge(g_abs, 3)
        nc.scalar.activation(lf[:], lf[:], ACT.Exp).then_inc(g_act, 1)
        nc.scalar.activation(gi[:], gi[:], ACT.Exp).then_inc(g_act, 1)
        nc.scalar.activation(t1[:], mm[:], ACT.Exp, scale=-1.0).then_inc(g_act, 1)
        nc.scalar.activation(dk[:], dk[:], ACT.Exp).then_inc(g_act, 1)

    def vector(self, dve):
        nc, g_abs, g_act, g_in, g_order = self.k.nc, self.steps, self.acted, self.loaded, self.ready
        order = Order(dve, self.order)
        gi, gf, lf, bb, mm, t1, rst, isf = self.tables
        bg, m0, mp, mn, bl, dk = self.small

        def chunks(x):
            return ((x[:, 0:SEQ].rearrange("p (c t) -> p c t", t=CHUNK), slice(0, 8), CHUNK),
                    (x[:, SEQ:TOK].rearrange("p (c t) -> p c t", t=DEC_T), slice(8, 16), DEC_T))

        dve.wait_ge(g_in, 96)
        order(nc.vector.tensor_scalar(gi[:], gi[:], bg[:, 0:1], None, ALU.add))
        order.step(nc.vector.tensor_scalar(gf[:], gf[:], bg[:, 1:2], None, ALU.add))
        nc.vector.scalar_tensor_tensor(t1[:], gf[:], -1.0, gf[:], ALU.mult, ALU.max).then_inc(g_abs, 1)
        dve.wait_ge(g_act, 1)
        nc.vector.tensor_scalar(t1[:], t1[:], 1.0, None, ALU.add).then_inc(g_abs, 1)
        dve.wait_ge(g_act, 2)
        order.step(nc.vector.scalar_tensor_tensor(lf[:], gf[:], 0.0, t1[:], ALU.min, ALU.subtract))
        order(nc.vector.tensor_tensor_scan(bb[:], rst[:], lf[:], 0.0, ALU.mult, ALU.add))
        dvl, dvt = lf[:, SEQ:].rearrange("p (c t) -> p c t", t=DEC_T), gi[:, SEQ:].rearrange("p (c t) -> p c t", t=DEC_T)
        order.step(nc.vector.tensor_tensor(mn[:, 0:8].unsqueeze(2), dvl[:, :, 0:1], m0[:, 0:8].unsqueeze(2), ALU.add))
        order(nc.vector.tensor_copy(t1[:], gi[:]))
        order(nc.vector.tensor_tensor(gf[:], lf[:], isf[:], ALU.add))
        order.then()
        order.step(nc.vector.tensor_tensor(t1[:, SEQ:].rearrange("p (c t) -> p c t", t=DEC_T)[:, :, 0:1],
                                           dvt[:, :, 0:1], mn[:, 0:8].unsqueeze(2), ALU.max))
        order.step(nc.vector.tensor_tensor_scan(mm[:], gf[:], t1[:], 0.0, ALU.add, ALU.max))
        order(nc.vector.memset(mp[:, 0:1], 0.0))
        for (x, cs, n), (y, _, _) in zip(chunks(mm), chunks(bb)):
            order(nc.vector.tensor_copy(mn[:, cs].unsqueeze(2), x[:, :, n - 1:n]))
            order(nc.vector.tensor_copy(bl[:, cs].unsqueeze(2), y[:, :, n - 1:n]))
        order.then()
        order(nc.vector.tensor_copy(mp[:, 1:8], mn[:, 0:7]))
        order(nc.vector.tensor_copy(mp[:, 8:16], m0[:, 0:8]))
        order(nc.vector.tensor_tensor(bl[:], bl[:], mn[:], ALU.subtract))
        order(nc.vector.tensor_tensor(gf[:], gi[:], bb[:], ALU.subtract))
        order.then()
        order(nc.vector.tensor_tensor(dk[:], bl[:], mp[:], ALU.add))
        order(nc.vector.tensor_tensor(bb[:], bb[:], mm[:], ALU.subtract))
        order.then()
        for (x, cs, n), (y, _, _), (z, _, _), (w, _, _) in zip(chunks(lf), chunks(bb), chunks(gi), chunks(gf)):
            bc = lambda q: q[:, cs].unsqueeze(2).to_broadcast([ML_H, 8, n])
            order(nc.vector.tensor_tensor(x, y, bc(mp), ALU.add))
            order(nc.vector.tensor_tensor(z, w, bc(bl), ALU.add))
        order.then()
        dve.sem_inc(g_abs, 1)
        dve.wait_ge(g_act, 6)
        dve.sem_inc(g_order, 1)


def project_first(k):
    nc, ins, outs = k.nc, k.ins, k.outs
    pr = Projection(k, "a", A_BLOCKS, A_W, C_I)
    mw_loaded = k.sems("memw_loaded", 2)
    m_done, m_copied, m_stored = k.sem("memkv_ready"), k.sem("memkv_copied"), k.sem("memkv_stored")
    with ExitStack() as st:
        k.bank = [k.ps(f"bank{j}", [P, 512], st) for j in range(P_BANKS)]
        mbank = [k.ps(f"mbank{j}", [P, 512], st) for j in range(2)]
        k.w = k.sb("w", [P, 2, KT, 512], at=st)
        k.pout = k.sb("pout", [P, P_BANKS, 512], at=st)
        mout = k.sb("mout", [P, 4, 512], at=st)
        gates = Gates(k, st)
        block = st.enter_context(nc.Block())

        @block.sync
        def _(sp):
            def memory_weights(j, name):
                sp.wait_ge(pr.free, A_BLOCKS + 1 + j)
                sp.dma_start(k.w[:, j, :, :], ins[name].rearrange("(c p) n -> p c n", p=P)
                             ).then_inc(mw_loaded[j], 16)

            def before_last():
                memory_weights(0, "w_mem_k")
                for j in range(P_BANKS):
                    sp.wait_ge(pr.stored[j], 16 * 3)
                gates.load(sp)

            pr.sync(sp, before_last)
            memory_weights(1, "w_mem_v")
            for j, name in enumerate(("prompt_mem_k", "prompt_mem_v")):
                for t in range(2):
                    sp.wait_ge(m_copied, 2 * j + t + 1)
                    sp.dma_start(outs[name][t * P:(t + 1) * P, :], mout[:, 2 * j + t, :]
                                 ).then_inc(m_stored, 16)
            gates.store(sp)
            sp.wait_ge(gates.stored, 16 * 8)
            sp.wait_ge(m_stored, 64)

        @block.vector
        def _(dve):
            gates.vector(dve)

        @block.scalar
        def _(act):
            pr.scalar(act)
            gates.scalar(act)
            for j in range(4):
                act.wait_ge(m_done, j + 1)
                nc.scalar.activation(mout[:, j, :], mbank[j % 2][:, :], ACT.Copy).then_inc(m_copied, 1)

        @block.tensor
        def _(pe):
            pr.credit(pe)
            pr.tensor(pe)
            for j in range(2):
                pe.wait_ge(mw_loaded[j], 16)
                for t in range(2):
                    if j:
                        pe.wait_ge(m_copied, t + 1)
                    for c in range(KT):
                        last = nc.tensor.matmul(mbank[t][:, :], k.memT[:, c, t * P:(t + 1) * P],
                                                k.w[:, j, c, :], start=c == 0, stop=c == KT - 1)
                    last.then_inc(m_done, 1)


def rotate(k):
    nc, ins, outs = k.nc, k.ins, k.outs
    n_in = 5
    loaded = k.sems("rot_loaded", 2)
    free_v, free_p, free_t = (k.sem(f"rot_free_by_{e}") for e in ("dve", "pool", "pe"))
    sa_done, ix_done = k.sem("sa_rotated"), k.sem("ix_rotated")
    turned, kept = k.sem("head_turned"), k.sem("head_kept")
    stored, passed = k.sems("rot_stored", 2), k.sem("pe_wait_passed")
    vstored = k.sem("v_stored")
    k.group_turned, k.sq_stored = k.sem("group_turned"), k.sem("sq_stored")
    sa_ord, ix_ord = k.sem("sa_rotary_order"), k.sem("ix_rotary_order")
    with ExitStack() as st:
        qk = k.sb("rot_qk", [P, 2, 2 * H, DH], at=st)
        ix = k.sb("rot_ix", [P, 2, IDX_H + 1, IDX_D], at=st)
        mq = k.sb("rot_mq", [P, 2, HW], at=st)
        cs = k.sb("rot_cs", [P, 2, 2, DH // 2], at=st)
        cs2 = k.sb("rot_cs2", [P, 2, 2, IDX_D // 2], at=st)
        rqk = k.sb("rqk", [P, 2, 2 * H, DH], at=st)
        rix = k.sb("rix", [P, 2, IDX_H + 1, IDX_D], at=st)
        ta = k.sb("rot_ta", [P, 4, 2 * H, DH // 2], at=st)
        tb = k.sb("rot_tb", [P, 4, IDX_H + 1, IDX_D // 2], at=st)
        keep = k.sb("rot_keep", [P, 2, T_SLOTS, P], at=st)
        banks = [k.ps(f"rbank{j}", [P, 4, P], st) for j in range(5)]
        block = st.enter_context(nc.Block())

        def tile(n, what):
            return (n * P, P) if what is None else (SEQ, NS)

        @block.sync
        def _(sp):
            sp.dma_start(outs["prompt_v"][:, :], k.proj[0:SEQ, C_SV:C_SV + HW]).then_inc(vstored, 16)
            sp.dma_start(outs["sample_v"][:, :], k.proj[SEQ:TOK, C_SV:C_SV + HW]).then_inc(vstored, 16)
            for n, u, i, what in pairs(sp, QT, "sample"):
                r0, r = tile(n, what)
                rs = bass.ds(r0, r) if what is None else slice(r0, r0 + r)
                for free in (free_v, free_p, free_t):
                    sp.wait_ge(free, n + 1)
                for dst, src in ((qk[0:r, u, :, :].rearrange("p h d -> p (h d)"), k.proj[rs, C_SQ:C_SV]),
                                 (ix[0:r, u, :, :].rearrange("p h d -> p (h d)"), k.proj[rs, C_IQ:C_IW]),
                                 (mq[0:r, u, :], k.proj[rs, C_MQ:C_MZ]),
                                 (cs[0:r, u, :, :], ins["rot128"][rs, :, :]),
                                 (cs2[0:r, u, :, :], ins["rot64"][rs, :, :])):
                    sp.dma_start(dst, src).then_inc(loaded[u], 16)
            sp.wait_ge(vstored, 32)

        def rotary(eng, order, x, c, o, t, n_heads, half, r):
            x1, x2 = x[0:r, :, 0:half], x[0:r, :, half:2 * half]
            cos = c[0:r, 0:1, :].to_broadcast([r, n_heads, half])
            sin = c[0:r, 1:2, :].to_broadcast([r, n_heads, half])
            order(eng.tensor_tensor(t[0:r, 0], x1, cos, ALU.mult))
            order(eng.tensor_tensor(t[0:r, 1], x2, sin, ALU.mult))
            order(eng.tensor_tensor(t[0:r, 2], x1, sin, ALU.mult))
            order(eng.tensor_tensor(t[0:r, 3], x2, cos, ALU.mult))
            order.then()
            order(eng.tensor_tensor(o[0:r, :, 0:half], t[0:r, 0], t[0:r, 1], ALU.subtract))
            order(eng.tensor_tensor(o[0:r, :, half:2 * half], t[0:r, 2], t[0:r, 3], ALU.add))
            order.then()

        @block.vector
        def _(dve):
            order = Order(dve, sa_ord)
            dve.sem_inc(free_v, 2)
            for n, u, i, what in pairs(dve, QT, "sample", order=order, per=12):
                r = tile(n, what)[1]
                dve.wait_ge(loaded[u], i * 16 * n_in + 16 * n_in)
                dve.wait_ge(stored[u], i * 64 + 64)
                dve.wait_ge(turned, n + 1)
                rotary(nc.vector, order, qk[:, u], cs[:, u], rqk[:, u], ta, 2 * H, DH // 2, r)
                dve.sem_inc(sa_done, 1)
                dve.sem_inc(free_v, 1)

        @block.gpsimd
        def _(pool):
            order = Order(pool, ix_ord)
            pool.sem_inc(free_p, 2)
            for n, u, i, what in pairs(pool, QT, "sample", order=order, per=12):
                r = tile(n, what)[1]
                pool.wait_ge(loaded[u], i * 16 * n_in + 16 * n_in)
                pool.wait_ge(stored[u], i * 64 + 64)
                pool.wait_ge(turned, n + 1)
                rotary(nc.gpsimd, order, ix[:, u], cs2[:, u], rix[:, u], tb, IDX_H + 1, IDX_D // 2, r)
                pool.sem_inc(ix_done, 1)
                pool.sem_inc(free_p, 1)

        @block.tensor
        def _(pe):
            pe.sem_inc(free_t, 2)
            pe.sem_inc(turned, 2)
            pe.sem_inc(kept, 5)
            for n, u, i, what in pairs(pe, QT, "sample"):
                r = tile(n, what)[1]
                for g in range(5):
                    pe.wait_ge(kept, 5 * n + g + 1)
                    if g == 0:
                        pe.wait_ge(loaded[u], i * 16 * n_in + 16 * n_in)
                        heads = [mq[0:r, u, h * DH:(h + 1) * DH] for h in range(H)]
                    elif g == 1:
                        pe.wait_ge(sa_done, n + 1)
                        heads = [rqk[0:r, u, h, :] for h in range(H)]
                    elif g == 2:
                        heads = [rqk[0:r, u, H + h, :] for h in range(H)]
                    elif g == 3:
                        pe.wait_ge(ix_done, n + 1)
                        heads = [rix[0:r, u, 2 * h:2 * h + 2, :].rearrange("p a d -> p (a d)")
                                 for h in range(IDX_H // 2)]
                    else:
                        heads = [rix[0:r, u, IDX_H, :]]
                    if g == 4:
                        pe.sem_inc(passed, 1)
                    for j, x in enumerate(heads):
                        last = nc.tensor.transpose(banks[g][0:x.shape[1], j, 0:r], x, k.ident[0:r, 0:r])
                    last.then_inc(k.group_turned, 1)
                pe.wait_ge(k.group_turned, 5 * n + 5)
                pe.sem_inc(turned, 1)
                pe.sem_inc(free_t, 1)

        @block.scalar
        def _(act):
            for u in range(2):
                act.sem_inc(stored[u], 64)
            slots = (T_MQ, T_Q, T_K, T_IQ, T_IK)
            for n, u, i, what in pairs(act, QT, "sample"):
                r0, r = tile(n, what)
                cols = bass.ds(r0, r) if what is None else slice(r0, r0 + r)
                act.wait_ge(stored[u], i * 64 + 64)
                for g, s in enumerate(slots):
                    act.wait_ge(k.group_turned, 5 * n + g + 1)
                    w, m = (4, P) if g < 4 else (1, IDX_D)
                    nc.scalar.activation(keep[0:m, u, s:s + w, 0:r], banks[g][0:m, 0:w, 0:r],
                                         ACT.Copy).then_inc(kept, 1)
                act.wait_ge(kept, 5 * n + 10)
                who = "prompt" if what is None else "sample"
                rows = cols if what is None else slice(0, NS)
                act.dma_start(outs[f"{who}_k"][rows, :], rqk[0:r, u, H:2 * H, :].rearrange("p h d -> p (h d)")
                              ).then_inc(stored[u], 16)
                act.dma_start(outs[f"{who}_kidx"][rows, :], rix[0:r, u, IDX_H, :]).then_inc(stored[u], 16)
                act.dma_start(k.headT[:, 0:T_IK, cols], keep[:, u, 0:T_IK, 0:r]).then_inc(stored[u], 16)
                if what is not None:
                    act.dma_start(k.sq[:, :], rqk[0:r, u, 0:H, :].rearrange("p h d -> p (h d)")
                                  ).then_inc(k.sq_stored, 16)
                    act.wait_ge(k.sq_stored, 16)
                act.dma_start(k.headT[0:IDX_D, T_IK, cols], keep[0:IDX_D, u, T_IK, 0:r]).then_inc(stored[u], 16)
            act.wait_ge(stored[0], 64 * (QT // 2 + 2))
            act.wait_ge(stored[1], 64 * (QT // 2 + 1))


S_COLS = PAST // 4 + DEC_T
MID = -3.15e38


def select(k):
    nc, ins = k.nc, k.ins
    pr = Projection(k, "b", B_BLOCKS, B_W, 0)
    S = k.sem
    const, wcol_in, small, iws_out = S("select_consts"), S("wcol_loaded"), S("select_small"), S("iws_stored")
    pages = k.queue_sems("pages_loaded", 2)
    pages_turned, kt_a, kt_v = S("pages_turned"), S("keysT_by_act"), S("keysT_by_dve")
    unit_turned, dotted, relu_s, summed = S("unit_turned"), S("unit_dotted"), S("unit_relu"), S("unit_summed")
    qz_ready, s_copied = S("qz_wz_ready"), S("decode_scores_copied")
    ki_in, q_in, q_free = S("kiT_loaded"), k.sems("qiT_loaded", 2), S("qiT_free")
    dots, relus, accs, biased = S("dots_ready"), S("relu_ready"), S("score_summed"), S("score_biased")
    order_sem, dve_passed, pool_passed = S("select_dve_order"), S("dve_wait_passed"), S("pool_wait_passed")
    sel_ready, (sel_out,) = S("selection_ready"), k.queue_sems("selection_stored", 1)
    rid_ready, cand_ready, adr_ready, gc_ready = S("rid_ready"), S("cand_ready"), S("adr_ready"), S("rid_clamped")
    rid_out, cand_out, vals_in, adr_out, adr_in, g1_done, g2_done = k.queue_sems("selected_dma", 7)
    k_in, k_free, qb_in = k.queue_sems("k_gathered", 4), S("k_free"), k.queue_sems("qb_loaded", 2)
    z_in, z_done, z_out = k.sems("z_loaded", 2), S("z_silu"), k.sems("z_stored", 2)
    qb_free, kidx_set = S("qb_free"), S("kidx_set")
    k.pti_in, k.dots_s = S("pti_loaded"), S("key_dots_ready")
    UNITS = 32
    with ExitStack() as st:
        bank = [k.ps(f"sbank{j}", [P, 512], st) for j in range(8)]
        k.bank = bank
        k.w = k.sb("w_b", [P, 2, KT, 512], at=st)
        k.pout = k.sb("pout_b", [P, P_BANKS, 512], at=st)
        ki = [k.w[:, u, :, :].rearrange("p a b -> p (a b)") for u in range(2)]
        sc = k.sb("prompt_scores", [P, 10, 512], at=st)
        kiT = k.sb("kiT", [P, SEQ], at=st)
        qiT = k.sb("qiT", [P, 2, 4, P], at=st)
        relu = k.sb("relu", [P, 4, 512], at=st)
        late = k.sb("late", [P, 2112], at=st)
        iw = k.sb("iw", [P, 6, IDX_H], at=st)
        ktT = k.pout[:, 0:4, :].rearrange("p (u a) (b c) -> p u (a b) c", u=2, c=P)
        qi4 = k.sb("qi4", [P, 2, 4, NS], at=st)
        qz = late[:, 0:DEC_B * P].rearrange("p (b c) -> p b c", c=P)
        wz = late[:, DEC_B * P:2 * DEC_B * P].rearrange("p (b c) -> p b c", c=P)
        rid = late[:, 0:S_COLS].bitcast(I32)
        newrid = k.sb("newrid", [P, DEC_T], I32, at=st)
        m8s = k.sb("m8s", [P, 8], at=st)
        c8s = k.sb("c8s", [P, 8], U32, at=st)
        c2s = k.sb("c2s", [NS, 8], U32, at=st)
        kidx = k.sb("kidx", [P, 4], I32, at=st)
        pick = k.sb("pick_sb", [P, 2, 8], at=st)
        wcol = k.sb("wcol", [P, 4], at=st)
        ktn = k.sb("ktn", [P, NS], at=st)
        rn = k.sb("rn", [P, 16], at=st)
        pti = k.sb("pti", [P, 4], I32, at=st)
        ss = k.sb("decode_scores", [P, S_COLS], at=st)
        nbias = k.sb("nbias", [P, DEC_T], at=st)
        kpos = k.sb("kpos_sb", [P, 512], at=st)
        qrel = k.sb("qrel_sb", [P, 2 * QT], at=st)
        slot0 = k.sb("slot0_sb", [P, 1], at=st)
        sstep = k.sb("sstep", [P, 32], at=st)
        rbase = k.sb("rbase", [P, 1], at=st)
        cbase = k.sb("cbase", [NS, 1], at=st)
        ptr = k.sb("ptr", [P, N_PAGES], I32, at=st)
        ptf = k.sb("ptf", [P, N_PAGES], at=st)
        vals = k.sb("vals", [P, TOPK], at=st)
        cidx = k.sb("cidx", [P, TOPK], U32, at=st)
        m8 = k.sb("m8", [P, 6, 8], at=st)
        v2 = relu[0:NS, 2:4, :].rearrange("p a b -> p (a b)")
        causal = relu[:, 0:2, :]
        p2 = k.sb("p2", [NS, TOPK], U32, at=st)
        m2 = k.sb("m2", [NS, 8], at=st)
        i1 = k.sb("i1", [P, 64], I32, at=st)
        i2 = k.sb("i2", [P, 64], I32, at=st)
        kg, qb, prod = sc[:, 0:4, :], sc[:, 4:6, :], sc[:, 6:8, :]
        block = st.enter_context(nc.Block())

        def items(eng):
            for j in range(2):
                yield j, j, 2 + j, j % 2, 0, None
            with eng.Fori(0, 2) as i:
                for u in range(2):
                    for f in range(2):
                        yield i * 4 + (2 + 2 * u + f), 2 + 2 * u + f, i * 2 + (4 + u), u, f, i

        @block.sync
        def _(sp):
            sp.dma_start(pti[:], ins["page_table"].rearrange("(p b) j -> (b j) p", b=2)).then_inc(k.pti_in, 16)
            for s2 in range(2):
                rows = slice(64 * s2, 64 * s2 + 64)
                for par in range(2):
                    sp.dma_start(qi4[rows, par, :, :], k.headT[64 * par:64 * par + 64, T_IQ:T_IK, SEQ:TOK]
                                 ).then_inc(const, 16)
                sp.dma_start(kiT[rows, :], k.headT[0:IDX_D, T_IK, 0:SEQ]).then_inc(ki_in, 16)
            sp.dma_start(ktn[0:64, :], k.headT[0:IDX_D, T_IK, SEQ:TOK]).then_inc(const, 16)
            sp.dma_start(pick[:, :, :], ins["pick"].rearrange("p (s c) -> p s c", s=2)).then_inc(const, 16)
            for b in range(DEC_B):
                sp.dma_start(k.iws[b, :, :].rearrange("h t -> t h"),
                             k.proj[SEQ + DEC_T * b:SEQ + DEC_T * (b + 1), C_IW:C_MQ]).then_inc(iws_out, 16)
            sp.dma_start(k.pt4[:, :, :], ins["page_table"].unsqueeze(1).to_broadcast([DEC_B, DEC_T, N_PAGES])
                         ).then_inc(iws_out, 16)
            sp.wait_ge(iws_out, 16 * (DEC_B + 1))
            for b2 in range(2):
                for s2 in range(2):
                    r = 64 * b2 + 32 * s2
                    sp.dma_start(wcol[r:r + 32, :], k.iws.rearrange("(p b) h t -> b (h t) p", b=2)[b2]
                                 ).then_inc(const, 16)
            for name, dst in (("new_bias", nbias), ("qrel", qrel), ("slot0", slot0), ("row_base", rbase),
                              ("cand_base", cbase)):
                sp.dma_start(dst[:], ins[name][:, :]).then_inc(small, 16)
            for name, dst in (("kpos", kpos), ("slot_step", sstep)):
                sp.dma_start(dst[:], ins[name][0:1, :].partition_broadcast(P)).then_inc(small, 16)
            sp.dma_start(newrid[:], ins["new_rid"][:, :]).then_inc(small, 16)
            sp.dma_start(iw[:, :, :], k.proj[2 * P:SEQ, C_IW:C_MQ].rearrange("(i p) h -> p i h", p=P)
                         ).then_inc(small, 16)
            for g in range(4):
                sp.dma_start(ptr[32 * g:32 * g + 32, :], k.pt4.rearrange("b t j -> (b t) j")).then_inc(small, 16)
            n = 0
            for tile, u in ((2, 0), (3, 1)):
                sp.dma_start(qiT[:, u, :, :], k.headT[:, T_IQ:T_IK, tile * P:(tile + 1) * P]).then_inc(q_in[u], 16)
            with sp.Fori(0, 2) as i:
                for u in range(2):
                    sp.wait_ge(q_free, i * 2 + u + 1)
                    sp.dma_start(qiT[:, u, :, :], k.headT[:, T_IQ:T_IK, bass.ds(i * 2 * P + (4 + u) * P, P)]
                                 ).then_inc(q_in[u], 16)
            pr.sync(sp)

        @block.gpsimd
        def _(pool):
            pool.wait_ge(k.pti_in, 16)
            for p in range(4):
                if p >= 2:
                    pool.wait_ge(pages_turned, p - 1)
                nc.gpsimd.indirect_dma_start(
                    out=ki[p % 2], out_offset=None, in_=ins["cache_kidx"][:, :],
                    in_offset=bass.IndirectOffsetOnAxis(ap=pti[:, p:p + 1], axis=0)).then_inc(pages[p % 2], 16)
            pool.wait_ge(rid_ready, 2)
            nc.gpsimd.dma_start(k.rid_d[:, :], rid).then_inc(rid_out, 16)
            pool.wait_ge(cand_ready, 1)
            for g in range(4):
                rows = slice(NS * g, NS * g + NS)
                nc.gpsimd.dma_start(k.cand[:, g, :], cidx[rows, :].bitcast(I32)).then_inc(cand_out, 16)
                nc.gpsimd.dma_start(v2[:, TOPK * g:TOPK * (g + 1)], vals[rows, :]).then_inc(vals_in, 16)
            pool.wait_ge(sel_ready, 12)
            tiles = [(0, 0), (1, 0), (2, 0), (3, 0)] + [(t, f) for t in range(4, QT) for f in range(2)]
            for m, (t, f) in enumerate(tiles):
                src = causal[:, m, :] if m < 2 else sc[:, m - 2, :]
                nc.gpsimd.dma_start(k.sel[t * P:(t + 1) * P, 512 * f:512 * f + 512], src).then_inc(sel_out, 16)
            pool.wait_ge(adr_ready, 1)
            nc.gpsimd.dma_start(k.adr.rearrange("(t c) -> t c", c=TOPK), p2[:].bitcast(I32)).then_inc(adr_out, 16)
            pool.wait_ge(adr_out, 16)
            with nc.allow_non_contiguous_dma("indices, one to a partition"):
                nc.gpsimd.dma_start(i1[:], k.adr.rearrange("(c p) -> p c", p=P)).then_inc(adr_in, 16)
            pool.wait_ge(adr_in, 16)
            pool.wait_ge(cand_out, 64)
            pool.wait_ge(rid_out, 16)
            for src, dst, table, done in ((i1, i2, k.cand.rearrange("t g (c o) -> (t g c) o", o=1), g1_done),
                                          (i2, k.rids, k.rid_d.rearrange("p (c o) -> (p c) o", o=1), g2_done)):
                for c in range(2 * NS):
                    nc.gpsimd.indirect_dma_start(
                        out=dst[:, c:c + 1], out_offset=None, in_=table,
                        in_offset=bass.IndirectOffsetOnAxis(ap=src[:, c:c + 1], axis=0)).then_inc(done, 16)
                pool.wait_ge(done, 16 * 2 * NS)
            pool.wait_ge(gc_ready, 1)
            pool.wait_ge(sel_out, 16 * 12)
            with pool.Fori(0, 16) as i:
                for c in range(4):
                    pool.wait_ge(k_free, i * 4 + c + 1)
                    nc.gpsimd.tensor_copy(kidx[:, c:c + 1], k.rowid[:, bass.ds(i * 4 + c, 1)]).then_inc(kidx_set, 1)
                    if c % 2 == 0:
                        pool.wait_ge(qb_free, i * 2 + c // 2 + 1)
                        nc.gpsimd.dma_start(qb[:, c // 2, :], k.sq[bass.ds(i * 2 + c // 2, 1), :].partition_broadcast(P)
                                            ).then_inc(qb_in[c // 2], 16)
                    pool.wait_ge(kidx_set, i * 4 + c + 1)
                    pool.sem_inc(pool_passed, 1)
                    nc.gpsimd.indirect_dma_start(
                        out=kg[:, c, :], out_offset=None, in_=ins["cache_k"][:, :],
                        in_offset=bass.IndirectOffsetOnAxis(ap=kidx[:, c:c + 1], axis=0)).then_inc(k_in[c], 16)

        @block.tensor
        def _(pe):
            def turn(n):
                p = n // 8
                if n % 8 == 0:
                    pe.wait_ge(pages[p % 2], 16 * (p // 2 + 1))
                if n:
                    pe.wait_ge(kt_a, n)
                for c in range(8):
                    if c == 4 and n:
                        pe.wait_ge(kt_v, n)
                    sp_ = (n % 8) * 8 + c
                    last = nc.tensor.transpose(bank[4 + c // 4][:, (c % 4) * P:(c % 4 + 1) * P],
                                               ki[p % 2][:, sp_ * P:(sp_ + 1) * P], k.ident[:])
                    if c % 4 == 3:
                        last.then_inc(unit_turned, 1)
                if n % 8 == 7:
                    pe.wait_ge(unit_turned, 2 * n + 2)
                    pe.sem_inc(pages_turned, 1)

            def dot(n):
                p = n // 8
                pe.wait_ge(kt_a, n + 1)
                pe.wait_ge(kt_v, n + 1)
                if n >= 2:
                    pe.wait_ge(relu_s, n - 1)
                for b2 in range(2):
                    last = nc.tensor.matmul(bank[6 + n % 2][:, :], qz[:, 2 * p + b2, :],
                                            ktT[:, n % 2, :, 64 * b2:64 * b2 + 64], start=b2 == 0, stop=b2 == 1)
                last.then_inc(dotted, 1)

            def total(n):
                pe.wait_ge(relu_s, n + 1)
                nc.tensor.matmul(bank[n % 4][:, :], wz[:, n // 4, :], relu[:, n % 2, :], start=n < 4,
                                 stop=n >= UNITS - 4).then_inc(summed, 1)

            pe.wait_ge(qz_ready, 1)
            for n in range(UNITS + 2):
                if n < UNITS:
                    turn(n)
                if 1 <= n <= UNITS:
                    dot(n - 1)
                if n >= 2:
                    total(n - 2)
            pe.wait_ge(relu_s, UNITS)
            for p in range(4):
                for b2 in range(2):
                    b = 2 * p + b2
                    last = nc.tensor.matmul(bank[6][:, 4 * p:4 * p + 4], qz[:, b, :],
                                            ktn[:, DEC_T * b:DEC_T * (b + 1)], start=b2 == 0, stop=b2 == 1)
            last.then_inc(dotted, 1)
            pe.wait_ge(relu_s, UNITS + 1)
            for p in range(4):
                last = nc.tensor.matmul(bank[7][:, 0:4], wz[:, 2 * p, :], rn[:, 4 * p:4 * p + 4],
                                        start=p == 0, stop=p == 3)
            last.then_inc(summed, 1)
            pr.credit(pe)
            pe.wait_ge(ki_in, 32)
            pe.wait_ge(s_copied, 5)
            pe.sem_inc(relus, 4)
            for m, mm, tile, u, f, i in items(pe):
                if f == 0:
                    pe.wait_ge(q_in[u], 16 if i is None else i * 16 + 32)
                for h in range(IDX_H):
                    rows = slice(64 * (h % 2), 64 * (h % 2) + 64)
                    pe.wait_ge(relus, m * 8 + h + 1)
                    last = nc.tensor.matmul(bank[h % 4][:, :], qiT[rows, u, h // 2, :],
                                            kiT[rows, 512 * f:512 * f + 512], start=True, stop=True)
                    last.then_inc(dots, 1)
                if f == 1 or i is None:
                    pe.wait_ge(dots, m * 8 + 8)
                    pe.sem_inc(q_free, 1)
            pe.wait_ge(relus, 84)
            pr.tensor(pe)

        @block.scalar
        def _(act):
            for n in range(UNITS):
                act.wait_ge(unit_turned, 2 * n + 1)
                if n >= 2:
                    act.wait_ge(dotted, n - 1)
                nc.scalar.activation(ktT[:, n % 2, 0:4, :].rearrange("p a b -> p (a b)"), bank[4][:, :],
                                     ACT.Copy).then_inc(kt_a, 1)
                if n:
                    act.wait_ge(dotted, n)
                    if n > 2:
                        act.wait_ge(summed, n - 2)
                    nc.scalar.activation(relu[:, (n - 1) % 2, :], bank[6 + (n - 1) % 2][:, :],
                                         ACT.Relu).then_inc(relu_s, 1)
            n = UNITS
            act.wait_ge(dotted, n)
            act.wait_ge(summed, n - 2)
            nc.scalar.activation(relu[:, (n - 1) % 2, :], bank[6 + (n - 1) % 2][:, :], ACT.Relu).then_inc(relu_s, 1)
            act.wait_ge(dotted, n + 1)
            nc.scalar.activation(rn[:], bank[6][:, 0:16], ACT.Relu).then_inc(relu_s, 1)
            act.wait_ge(summed, UNITS)
            for m, mm, tile, u, f, i in items(act):
                for h in range(IDX_H):
                    act.wait_ge(dots, m * 8 + h + 1)
                    act.wait_ge(accs, m * 8 + h + 1)
                    nc.scalar.activation(relu[:, h % 4, :], bank[h % 4][:, :], ACT.Relu).then_inc(relus, 1)

            def silu_of_groups():
                act.wait_ge(accs, 84)
                zslot = [qiT[:, c, :, :].rearrange("p a b -> p (a b)") for c in range(2)]
                with act.Fori(0, QT) as i:
                    places = [k.proj[bass.ds(i * P, P), c:c + HW] for c in (C_SZ, C_MZ)]
                    for c, at in enumerate(places):
                        act.wait_ge(z_out[c], i * 16 + 16)
                        act.dma_start(zslot[c], at).then_inc(z_in[c], 16)
                    for c, at in enumerate(places):
                        act.wait_ge(z_in[c], i * 16 + 16)
                        nc.scalar.activation(zslot[c], zslot[c], ACT.Silu).then_inc(z_done, 1)
                        act.wait_ge(z_done, i * 2 + (c + 1))
                        act.dma_start(at, zslot[c]).then_inc(z_out[c], 16)
                for c in range(2):
                    act.wait_ge(z_out[c], 16 * (QT + 1))

            for c in range(2):
                act.sem_inc(z_out[c], 16)
            pr.between = [silu_of_groups]
            pr.scalar(act, (3 * ML_W // B_W // 2, ACT.Copy), (ML_W // B_W // 2, ACT.Sigmoid),
                      (ML_W // B_W // 2, ACT.Silu))

        @block.vector
        def _(dve):
            order = Order(dve, order_sem, dve_passed)
            order(nc.vector.memset(qz[:], 0.0))
            order(nc.vector.memset(wz[:], 0.0))
            order(nc.vector.memset(ktn[64:128, :], 0.0))
            dve.wait_ge(const, 16 * 10)
            order.then()
            for b in range(DEC_B):
                for s2 in range(2):
                    rows = slice(64 * s2, 64 * s2 + 64)
                    c0 = 64 * (b % 2) + 32 * s2
                    order(nc.vector.tensor_copy(
                        qz[rows, b, c0:c0 + 32].rearrange("p (a q t) -> p q a t", q=2, t=DEC_T),
                        qi4[rows, :, :, DEC_T * b:DEC_T * (b + 1)]))
            for p in range(4):
                for half in range(2):
                    for s2 in range(2):
                        c0 = 32 * (2 * half + s2) + 8 * p
                        order(nc.vector.tensor_scalar(wz[:, 2 * p + half, c0:c0 + 8], pick[:, s2, :],
                                                      wcol[:, p:p + 1], None, ALU.mult))
            order.then()
            dve.sem_inc(qz_ready, 1)
            for n in range(UNITS):
                dve.wait_ge(unit_turned, 2 * n + 2)
                if n >= 2:
                    dve.wait_ge(dotted, n - 1)
                nc.vector.tensor_copy(ktT[:, n % 2, 4:8, :].rearrange("p a b -> p (a b)"),
                                      bank[5][:, :]).then_inc(kt_v, 1)
            dve.wait_ge(summed, UNITS + 1)
            dve.wait_ge(small, 16 * 13)
            for j in range(4):
                nc.vector.tensor_copy(ss[:, 512 * j:512 * (j + 1)], bank[j][:, :]).then_inc(s_copied, 1)
            nc.vector.tensor_tensor(ss[:, S_COLS - DEC_T:], bank[7][:, 0:4], nbias[:], ALU.add).then_inc(s_copied, 1)
            order(nc.vector.tensor_scalar(iw[:], iw[:], IDX_SCALE, None, ALU.mult))
            order(nc.vector.tensor_scalar(ptf[:], ptr[:], float(PAGE), slot0[:], ALU.mult, ALU.add))
            order.then()
            nc.vector.tensor_tensor(rid[:, 0:PAST // 4].rearrange("p (s j) -> p s j", j=N_PAGES),
                                    ptf[:].unsqueeze(1).to_broadcast([P, 32, N_PAGES]),
                                    sstep[:].unsqueeze(2).to_broadcast([P, 32, N_PAGES]),
                                    ALU.add).then_inc(rid_ready, 1)
            nc.vector.tensor_copy(rid[:, S_COLS - DEC_T:], newrid[:]).then_inc(rid_ready, 1)
            dve.sem_inc(accs, 4)
            for m, mm, tile, u, f, i in items(dve):
                dst = sc[:, mm, :] if i is None else sc[:, bass.ds(m, 1), :].rearrange("p a b -> p (a b)")
                if i is None:
                    qr = qrel[:, 2 * tile + f:2 * tile + f + 1]
                    w = lambda h: iw[:, tile - 2, h:h + 1]
                else:
                    qr = qrel[:, bass.ds(tile * 2 + f, 1)]
                    w = lambda h: iw[:, bass.ds(tile - 2, 1), h:h + 1].rearrange("p a b -> p (a b)")
                nc.vector.tensor_scalar(dst, kpos[:], qr, NEG, ALU.is_gt, ALU.mult).then_inc(biased, 1)
                dve.wait_ge(biased, m + 1)
                for h in range(IDX_H):
                    dve.wait_ge(relus, m * 8 + h + 5)
                    if h:
                        dve.wait_ge(accs, m * 8 + h + 4)
                    nc.vector.scalar_tensor_tensor(dst, relu[:, h % 4, :], w(h), dst, ALU.mult,
                                                   ALU.add).then_inc(accs, 1)
            dve.wait_ge(accs, 84)
            for t in range(2):
                nc.vector.tensor_scalar(causal[:, t, :], kpos[:], qrel[:, 2 * t:2 * t + 1], NEG, ALU.is_gt,
                                        ALU.mult).then_inc(sel_ready, 1)
            dve.wait_ge(s_copied, 5)
            for i in order.loop(TOPK // 8, 5):
                order(nc.vector.max(m8s[:], ss[:]))
                order.then_plain()
                order(nc.vector.max_index(c8s[:], m8s[:], ss[:]))
                order(nc.vector.tensor_copy(vals[:, bass.ds(i * 8, 8)], m8s[:]))
                order.then_plain()
                order(nc.vector.match_replace(out=ss[:], in_to_replace=m8s[:], in_values=ss[:], imm_value=TAKEN))
                order(nc.vector.tensor_copy(cidx[:, bass.ds(i * 8, 8)], c8s[:]))
                order.then()
            nc.vector.tensor_scalar(cidx[:].bitcast(I32), cidx[:], rbase[:], None, ALU.add).then_inc(cand_ready, 1)
            spans = [sc[:, 0, :], sc[:, 1, :]] + [
                sc[:, 2 * j:2 * j + 2, :].rearrange("p a b -> p (a b)") for j in range(1, 5)]
            for i in order.loop(TOPK // 8, 12):
                for j, x in enumerate(spans):
                    order(nc.vector.max(m8[:, j, :], x))
                order.then_plain()
                for j, x in enumerate(spans):
                    order(nc.vector.match_replace(out=x, in_to_replace=m8[:, j, :], in_values=x, imm_value=TAKEN))
                order.then()
            for m in range(10):
                nc.vector.tensor_scalar(sc[:, m, :], sc[:, m, :], MID, NEG, ALU.is_ge, ALU.mult).then_inc(sel_ready, 1)
            dve.wait_ge(vals_in, 64)
            for i in order.loop(TOPK // 8, 4):
                order(nc.vector.max(m2[:], v2))
                order.then_plain()
                order(nc.vector.max_index(c2s[:], m2[:], v2))
                order.then_plain()
                order(nc.vector.match_replace(out=v2, in_to_replace=m2[:], in_values=v2, imm_value=TAKEN))
                order(nc.vector.tensor_copy(p2[:, bass.ds(i * 8, 8)], c2s[:]))
                order.then()
            nc.vector.tensor_scalar(p2[:].bitcast(I32), p2[:], cbase[:], None, ALU.add).then_inc(adr_ready, 1)
            dve.wait_ge(g2_done, 16 * 64)
            order(nc.vector.tensor_scalar(k.rbias[:], k.rids[:], float(N_POOL * PAGE), NEG, ALU.is_ge, ALU.mult))
            order(nc.vector.tensor_scalar(k.rowid[:], k.rids[:], float(N_POOL * PAGE - 1), None, ALU.min))
            order.then()
            dve.sem_inc(gc_ready, 1)
            dve.sem_inc(k_free, 4)
            dve.sem_inc(qb_free, 2)
            dve.sem_inc(k.dots_s, 2)
            with dve.Fori(0, 16) as i:
                for c in range(4):
                    q = c // 2
                    if c % 2 == 0:
                        dve.wait_ge(qb_in[q], i * 16 + 16)
                    dve.wait_ge(k_in[c], i * 16 + 16)
                    dve.wait_ge(k.dots_s, i * 4 + c + 1)
                    nc.vector.tensor_tensor(prod[:, c % 2, :], kg[:, c, :], qb[:, q, :], ALU.mult).then_inc(k_free, 1)
                    dve.wait_ge(k_free, i * 4 + c + 5)
                    nc.vector.tensor_reduce(
                        k.sck[:, c % 2, bass.ds(i * 8 + 4 * q, 4)],
                        prod[:, c % 2, :].rearrange("p (h d) -> p h d", h=H), AX, ALU.add).then_inc(k.dots_s, 1)
                    if c % 2:
                        dve.sem_inc(qb_free, 1)


SCALE = DH ** -0.5


class Attention:

    def __init__(self, k, sems, t0, tiles, width, slot_q, biased, col_z, col_out, before):
        self.k, self.s, self.t0, self.tiles, self.width = k, sems, t0, tiles, width
        self.slot_q, self.biased, self.cz, self.co = slot_q, biased, col_z, col_out
        self.tb = before

    def load(self, sp, t, u):
        k, s = self.k, self.s
        rows = bass.ds(t * P + self.t0 * P, P)
        sp.wait_ge(s.tile_free, t + self.tb + 1)
        sp.dma_start(k.qT[:, u, :, :], k.headT[:, self.slot_q:self.slot_q + H, rows]).then_inc(s.loaded[u], 16)
        sp.dma_start(k.z[:, u, :], k.proj[rows, self.cz:self.cz + HW]).then_inc(s.loaded[u], 16)
        if self.biased:
            sp.dma_start(k.bias[:, u, 0:self.width], k.sel[rows, 0:self.width]).then_inc(s.bias_in[u], 16)

    def store(self, sp, t, u):
        k, s = self.k, self.s
        sp.wait_ge(s.finished, t * H + (self.tb * H + H))
        sp.dma_start(k.hcat[bass.ds(t * P + self.t0 * P, P), self.co:self.co + HW],
                     k.ho[:, u, :]).then_inc(s.ho_stored[u], 16)

    def sync(self, sp):
        n = self.tiles
        self.load(sp, 0, 0)
        with sp.Fori(0, n // 2 - 1) as i:
            for u in range(2):
                self.load(sp, i * 2 + (u + 1), 1 - u)
                self.store(sp, i * 2 + u, u)
        self.load(sp, n - 1, 1)
        self.store(sp, n - 2, 0)
        self.store(sp, n - 1, 1)

    def tensor(self, pe):
        k, s, nc, w = self.k, self.s, self.k.nc, self.width
        kT, v = (k.kT, k.v) if self.biased else (k.mkT, k.mv)
        nb = (w + 511) // 512
        base = self.tb * H
        with pe.Fori(0, self.tiles // 2) as i:

            def dots(j):
                u, h = j // H, j % H
                if h == 0:
                    pe.wait_ge(s.loaded[u], i * 32 + (16 * self.tb + 32))
                pe.wait_ge(s.read, i * 8 + (j + base + 1))
                for b in range(nb):
                    c = min(512, w - 512 * b)
                    last = nc.tensor.matmul(k.bank[2 * (j % 2) + b][:, 0:c], k.qT[:, u, h, :],
                                            kT[:, h, 512 * b:512 * b + c], start=True, stop=True)
                last.then_inc(s.dotted, 1)

            def turn(j):
                pe.wait_ge(s.p_ready, i * 8 + (j + base + 1))
                pe.wait_ge(s.kept_a, i * 8 + (j + base + 1))
                pe.wait_ge(s.kept_v, i * 8 + (j + base + 1))
                for c in range(w // P):
                    last = nc.tensor.transpose(k.bank[4 + c // 4][:, c % 4 * P:(c % 4 + 1) * P],
                                               k.p[:, j % 2, c * P:(c + 1) * P], k.ident[:])
                last.then_inc(s.turned, 1)

            def mix(j):
                pe.wait_ge(s.kept_a, i * 8 + (j + base + 2))
                if w > 512:
                    pe.wait_ge(s.kept_v, i * 8 + (j + base + 2))
                pe.wait_ge(s.o_free, i * 8 + (j + base + 1))
                h = j % H
                for c in range(w // P):
                    last = nc.tensor.matmul(k.bank[6 + j % 2][:, 0:DH], k.pT[:, j % 2, c * P:(c + 1) * P],
                                            v[:, c, h * DH:(h + 1) * DH], start=c == 0, stop=c == w // P - 1)
                last.then_inc(s.mixed, 1)

            dots(0)
            for j in range(2 * H + 1):
                if j + 1 < 2 * H:
                    dots(j + 1)
                if j < 2 * H:
                    turn(j)
                if j:
                    mix(j - 1)

    def scalar(self, act):
        k, s, nc, w = self.k, self.s, self.k.nc, self.width
        base = self.tb * H
        with act.Fori(0, self.tiles // 2) as i:

            def weigh(j):
                u, h = j // H, j % H
                act.wait_ge(s.max_ready, i * 8 + (j + base + 1))
                act.wait_ge(s.p_free, i * 8 + (j + base + 1))
                src = k.lg[:, j % 2, 0:w] if self.biased else k.bank[2 * (j % 2)][:, 0:w]
                nc.scalar.activation(k.p[:, j % 2, 0:w], src, ACT.Exp, bias=k.nm[:, j % 2:j % 2 + 1],
                                     scale=1.0 if self.biased else SCALE,
                                     accum_out=k.rs[:, j % 2:j % 2 + 1]).then_inc(s.p_ready, 1)

            def keep(j):
                act.wait_ge(s.turned, i * 8 + (j + base + 1))
                act.wait_ge(s.mixed, i * 8 + (j + base + 1))
                c = min(w, 512)
                nc.scalar.activation(k.pT[:, j % 2, 0:c], k.bank[4][:, 0:c], ACT.Copy).then_inc(s.kept_a, 1)

            for j in range(2 * H + 1):
                if j < 2 * H:
                    weigh(j)
                if j:
                    keep(j - 1)

    def vector(self, dve, order):
        k, s, nc, w = self.k, self.s, self.k.nc, self.width
        base = self.tb * H
        nb = (w + 511) // 512
        per = 2 * H * ((nb if self.biased else 1) + 1)
        for i in order.loop(self.tiles // 2, per):

            def logits(j):
                u, q = j // H, j % 2
                dve.wait_ge(s.dotted, i * 8 + (j + base + 1))
                if self.biased:
                    if j % H == 0:
                        dve.wait_ge(s.bias_in[u], i * 16 + (8 * self.tb + 16))
                    for b in range(nb):
                        c = slice(512 * b, min(w, 512 * b + 512))
                        order(nc.vector.scalar_tensor_tensor(
                            k.lg[:, q, c], k.bank[2 * q + b][:, 0:c.stop - c.start], SCALE,
                            k.bias[:, u, c], ALU.mult, ALU.add))
                    order.then()
                    dve.sem_inc(s.read, 1)
                    nc.vector.tensor_reduce(k.nm[:, q:q + 1], k.lg[:, q, 0:w], AX, ALU.max,
                                            negate=True).then_inc(s.max_ready, 1)
                else:
                    order.step(nc.vector.tensor_reduce(k.mx[:, q:q + 1], k.bank[2 * q][:, 0:w], AX, ALU.max))
                    nc.vector.tensor_scalar(k.nm[:, q:q + 1], k.mx[:, q:q + 1], -SCALE, None,
                                            ALU.mult).then_inc(s.max_ready, 1)

            def keep(j):
                q = j % 2
                dve.wait_ge(s.turned, i * 8 + (j + base + 1))
                if w > 512:
                    dve.wait_ge(s.mixed, i * 8 + (j + base + 1))
                    nc.vector.tensor_copy(k.pT[:, q, 512:w], k.bank[5][:, 0:w - 512]).then_inc(s.kept_v, 1)
                else:
                    dve.sem_inc(s.kept_v, 1)
                dve.wait_ge(s.p_ready, i * 8 + (j + base + 1))
                if not self.biased:
                    dve.sem_inc(s.read, 1)
                order.step(nc.vector.reciprocal(k.rr[:, q:q + 1], k.rs[:, q:q + 1]))
                dve.sem_inc(s.p_free, 1)

            def finish(j):
                u, h, q = j // H, j % H, j % 2
                dve.wait_ge(s.mixed, i * 8 + (j + base + 3))
                hd = slice(h * DH, (h + 1) * DH)
                if h == 0:
                    dve.wait_ge(s.loaded[u], i * 32 + (16 * self.tb + 32))
                    dve.wait_ge(s.ho_stored[u], i * 16 + (8 * self.tb + 16))
                nc.vector.scalar_tensor_tensor(k.ho[:, u, hd], k.bank[6 + q][:, 0:DH], k.rr[:, q:q + 1],
                                               k.z[:, u, hd], ALU.mult, ALU.mult).then_inc(s.finished, 1)
                dve.wait_ge(s.finished, i * 8 + (j + base + 1))
                dve.sem_inc(s.o_free, 1)

            for j in range(2 * H + 2):
                if j < 2 * H:
                    logits(j)
                if 1 <= j <= 2 * H:
                    keep(j - 1)
                if j >= 2:
                    finish(j - 2)
                    if (j - 2) % H == H - 1:
                        dve.sem_inc(s.tile_free, 1)


class Signals:
    pass


def attend(k):
    nc, ins, outs = k.nc, k.ins, k.outs
    S = k.sem
    s = Signals()
    s.tile_free, s.finished, s.read, s.dotted = S("tile_free"), S("head_finished"), S("dots_read"), S("dots_done")
    s.p_ready, s.kept_a, s.kept_v, s.turned = S("p_ready"), S("pT_by_act"), S("pT_by_dve"), S("p_turned")
    s.o_free, s.mixed = S("o_free"), S("pv_done")
    s.max_ready, s.p_free = S("max_ready"), S("p_free")
    s.loaded, s.bias_in, s.ho_stored = k.sems("tile_loaded", 2), k.sems("bias_loaded", 2), k.sems("ho_stored", 2)
    keys_in, mem_in, order_sem = S("keys_loaded"), S("mem_loaded"), S("attend_order")
    new_stored, small_in = S("new_kv_stored"), S("decode_small_loaded")
    mk_turned, mk_kept = S("memk_turned"), S("memk_kept")
    lk_ready, lk_turned, pd_max, pd_exp, pd_ready, pd_turned = (
        S("dec_logits"), S("dec_logits_turned"), S("dec_max"), S("dec_exp"), S("dec_p_ready"), S("dec_p_turned"))
    mkd_in, mkd_free, qz_ready = k.sems("dec_memk_loaded", 2), S("dec_memk_free"), S("dec_query_slot")
    mkd_turned, mkd_kept, mdots = S("dec_memk_turned"), S("dec_memk_kept"), S("dec_mem_dots")
    pm_max, pm_exp, pm_ready, pm_turned, pm_kept = (
        S("dec_mem_max"), S("dec_mem_exp"), S("dec_mem_p"), S("dec_mem_p_turned"), S("dec_mem_p_kept"))
    mvd_in, v_in = S("dec_memv_loaded"), k.queue_sems("v_gathered", 32)
    pz_ready, pz_used, dec_clear, closed = S("p_slot_ready"), S("p_slot_used"), S("dec_banks_read"), S("dec_sum_closed")
    out_ready, out_mid, out_in, out_st, ed_ready = (
        S("dec_out"), S("dec_out_turned"), S("dec_out_loaded"), S("dec_out_stored"), S("dec_gate_exp"))
    N_B, N_C = 2 * NS, 2 * DEC_B
    with ExitStack() as st:
        bank = k.bank = [k.ps(f"abank{j}", [P, 512], st) for j in range(8)]
        k.kT, k.v = k.sb("kT", [P, H, SEQ], at=st), k.sb("v", [P, QT, HW], at=st)
        k.mkT, k.mv = k.sb("mkT", [P, H, N_MEM], at=st), k.sb("mv", [P, 2, HW], at=st)
        k.qT, k.z = k.sb("qT", [P, 2, H, P], at=st), k.sb("z", [P, 2, HW], at=st)
        k.bias, k.lg = k.sb("bias", [P, 2, SEQ], at=st), k.sb("lg", [P, 2, SEQ], at=st)
        mk = k.lg[:, 0, :].rearrange("p (c n) -> p c n", c=2)
        k.p, k.pT = k.sb("p", [P, 2, SEQ], at=st), k.sb("pT", [P, 2, SEQ], at=st)
        k.ho = k.sb("ho", [P, 2, HW], at=st)
        k.nm, k.mx, k.rs, k.rr = (k.sb(x, [P, 2], at=st) for x in ("nm", "mx", "rs", "rr"))
        VR = 32
        vg = k.sb("vg", [P, VR, HW], at=st)
        mvd = vg[:, 0:N_C, :]
        lk, pdT, pmT = (k.sb(x, [P, 2, P], at=st) for x in ("lk", "pdT", "pmT"))
        lt, pd = k.sb("lt", [P, TOPK + DEC_T], at=st), k.sb("pd", [P, TOPK + DEC_T], at=st)
        qr, kn, vn = k.sb("qr", [P, DH], at=st), k.sb("kn", [P, DEC_T, DH], at=st), k.sb("vn", [P, DEC_T, DH], at=st)
        nprod, nd = k.sb("nprod", [P, DEC_T, DH], at=st), k.sb("nd", [P, DEC_T], at=st)
        nid, eq = k.sb("nid", [P, DEC_T, N_B], at=st), k.sb("eq", [P, DEC_T, N_B], at=st)
        eqh = k.sb("eqh", [P, DEC_T * NS, H], at=st)
        ones, hm, stat = k.sb("ones", [P, 2], at=st), k.sb("hm", [P, H], at=st), k.sb("dec_stats", [P, 8], at=st)
        pz, zero = k.sb("pz", [P, 4, P], at=st), k.sb("zero", [P, P], at=st)
        mqT, mkd = k.sb("mqT", [P, H, NS], at=st), k.sb("mkd", [P, 2, 2, HW], at=st)
        mkdT, pm = k.sb("mkdT", [P, 2, N_MEM], at=st), k.sb("pm", [P, N_MEM], at=st)
        ob, oc = k.sb("ob", [P, DH], at=st), k.sb("oc", [P, DH], at=st)
        od, zd, ed = k.sb("od", [NS, 2, HW], at=st), mkd[0:NS, 0, :, :], mkd[0:NS, 1, :, :]
        runs = [Attention(k, s, 0, 4, 512, T_Q, True, C_SZ, ML_W, 0),
                Attention(k, s, 4, 4, 1024, T_Q, True, C_SZ, ML_W, 4),
                Attention(k, s, 0, 8, N_MEM, T_MQ, False, C_MZ, ML_W + HW, 8)]
        TILES = 16
        block = st.enter_context(nc.Block())

        @block.sync
        def _(sp):
            for t in range(DEC_T):
                for dst, src in ((k.kn4, outs["sample_k"]), (k.vn4, outs["sample_v"])):
                    sp.dma_start(dst[t, :, :, :], src.rearrange("(b t) c -> b t c", t=DEC_T)[:, t:t + 1, :]
                                 .to_broadcast([DEC_B, DEC_T, HW])).then_inc(new_stored, 16)
            sp.dma_start(mk, outs["prompt_mem_k"].rearrange("(c p) n -> p c n", p=P)).then_inc(mem_in, 16)
            sp.dma_start(k.mv[:, :, :], outs["prompt_mem_v"].rearrange("(c p) n -> p c n", p=P)).then_inc(mem_in, 16)
            sp.dma_start(nid[:, :, :].rearrange("p a b -> p (a b)"), ins["new_ids"][0:1, :].partition_broadcast(P)
                         ).then_inc(small_in, 16)
            sp.dma_start(hm[:], ins["head_pick"][:, :]).then_inc(small_in, 16)
            sp.dma_start(qr[:], k.sq.rearrange("t (h d) -> (t h) d", h=H)).then_inc(small_in, 16)
            sp.dma_start(mqT[:, :, :], k.headT[:, T_MQ:T_MQ + H, SEQ:TOK]).then_inc(small_in, 16)
            sp.wait_ge(new_stored, 16 * 2 * DEC_T)
            for dst, src in ((kn, k.kn4), (vn, k.vn4)):
                for t in range(DEC_T):
                    sp.dma_start(dst[:, t, :], src[t].rearrange("b t (h d) -> (b t h) d", h=H)).then_inc(small_in, 16)
            with sp.Fori(0, DEC_B // 2) as i:
                for u in range(2):
                    sp.wait_ge(mkd_free, i * 2 + u + 1)
                    sp.dma_start(mkd[:, u, :, :], ins["cache_mem_k"][bass.ds(i * 2 + u, 1), :, :]
                                 .rearrange("o (c p) n -> p (o c) n", p=P)).then_inc(mkd_in[u], 16)
            for b in range(DEC_B):
                sp.dma_start(mvd[:, 2 * b:2 * b + 2, :], ins["cache_mem_v"][b].rearrange("(c p) n -> p c n", p=P)
                             ).then_inc(mvd_in, 16)
            sp.dma_start(k.kT[:, :, :], k.headT[:, T_K:T_K + H, 0:SEQ]).then_inc(keys_in, 16)
            sp.dma_start(k.v[:, :, :], outs["prompt_v"].rearrange("(c p) n -> p c n", p=P)).then_inc(keys_in, 16)
            for r in runs:
                r.sync(sp)
            for j, c in enumerate((C_SZ, C_MZ)):
                sp.dma_start(zd[:, j, :], k.proj[SEQ:TOK, c:c + HW]).then_inc(out_in, 16)
            for j, o in enumerate((oc, ob)):
                sp.wait_ge(out_ready, j + 1)
                sp.dma_start(k.odec[1 - j].rearrange("t (h d) -> (t h) d", h=H), o[:]).then_inc(out_mid, 16)
            sp.wait_ge(out_mid, 32)
            sp.dma_start(od[:, :, :], k.odec.rearrange("j t c -> t j c")).then_inc(out_in, 16)
            sp.wait_ge(out_ready, 3)
            sp.dma_start(k.hcat[SEQ:TOK, ML_W:], od[:, :, :].rearrange("t j c -> t (j c)")).then_inc(out_st, 16)
            sp.wait_ge(out_st, 16)
            for u in range(2):
                sp.wait_ge(s.ho_stored[u], 16 * (TILES // 2 + 1))

        @block.gpsimd
        def _(pool):
            for c in range(N_B):
                if c == 0:
                    pool.wait_ge(pz_used, 4 + N_C)
                if c >= VR:
                    pool.wait_ge(pz_used, 4 + N_C + c - VR + 1)
                nc.gpsimd.indirect_dma_start(
                    out=vg[:, c % VR, :], out_offset=None, in_=ins["cache_v"][:, :],
                    in_offset=bass.IndirectOffsetOnAxis(ap=k.rowid[:, c:c + 1], axis=0)).then_inc(v_in[c % VR], 16)

        @block.tensor
        def _(pe):
            pe.wait_ge(mem_in, 32)
            for h in range(H):
                for c in range(2):
                    last = nc.tensor.transpose(bank[h // 2][:, 256 * (h % 2) + P * c:256 * (h % 2) + P * c + P],
                                               mk[:, c, h * DH:(h + 1) * DH], k.ident[:])
            last.then_inc(mk_turned, 1)
            pe.wait_ge(lk_ready, 1)
            for c in range(2):
                nc.tensor.transpose(bank[2][:, c * P:(c + 1) * P], lk[:, c, :], k.ident[:])
            for n in range(DEC_T):
                last = nc.tensor.matmul(bank[3][:, n:n + 1],
                                        eqh[:, NS * n:NS * (n + 1), :].rearrange("p a b -> p (a b)"),
                                        ones[:, 0:1], start=True, stop=True)
            last.then_inc(lk_turned, 1)
            pe.wait_ge(pd_ready, 1)
            for c in range(2):
                last = nc.tensor.transpose(bank[2][:, c * P:(c + 1) * P], pd[:, c * P:(c + 1) * P], k.ident[:])
            last.then_inc(pd_turned, 1)
            def empty(out, rhs, start):
                return nc.tensor.matmul(out, zero[:], rhs, start=start, stop=not start, skip_group_check=True)

            empty(bank[4][:, 0:N_MEM], k.mv[:, 0, 0:N_MEM], True)
            pe.sem_inc(mkd_free, 2)
            pe.sem_inc(mdots, 2)
            with pe.Fori(0, DEC_B // 2) as i:

                def turn(n):
                    u, h = n // H, n % H
                    if h == 0:
                        pe.wait_ge(mkd_in[u], i * 16 + 16)
                    pe.wait_ge(mkd_kept, i * 8 + (n + 1))
                    for c in range(2):
                        last = nc.tensor.transpose(bank[5 + n % 2][:, c * P:(c + 1) * P],
                                                   mkd[:, u, c, h * DH:(h + 1) * DH], k.ident[:])
                    last.then_inc(mkd_turned, 1)
                    if h == H - 1:
                        pe.wait_ge(mkd_turned, i * 8 + (n + 1))
                        pe.sem_inc(mkd_free, 1)

                turn(0)
                for n in range(2 * H):
                    if n + 1 < 2 * H:
                        turn(n + 1)
                    pe.wait_ge(mkd_kept, i * 8 + (n + 3))
                    pe.wait_ge(qz_ready, i * 8 + (n + 1))
                    nc.tensor.matmul(bank[4][:, 0:N_MEM], pz[:, n % 2, :], mkdT[:, n % 2, :], start=False,
                                     stop=False, skip_group_check=True).then_inc(mdots, 1)
            empty(bank[4][:, 0:N_MEM], k.mv[:, 0, 0:N_MEM], False).then_inc(mdots, 1)
            pe.wait_ge(pm_ready, 1)
            pe.wait_ge(mkd_kept, 2 + DEC_B * H)
            for c in range(2):
                last = nc.tensor.transpose(bank[5][:, c * P:(c + 1) * P], pm[:, c * P:(c + 1) * P], k.ident[:])
            last.then_inc(pm_turned, 1)
            empty(bank[6][:, :], k.mv[:, 0, :], True)
            pe.sem_inc(pz_used, 4)
            pe.wait_ge(mvd_in, 16 * DEC_B)
            with pe.Fori(0, N_C // 4) as i:
                for c in range(4):
                    pe.wait_ge(pz_ready, i * 4 + (c + 1))
                    nc.tensor.matmul(bank[6][:, :], pz[:, c, :], mvd[:, bass.ds(i * 4 + c, 1), :]
                                     .rearrange("p a b -> p (a b)"), start=False, stop=False,
                                     skip_group_check=True).then_inc(pz_used, 1)
            empty(bank[6][:, :], k.mv[:, 0, :], False).then_inc(closed, 1)
            pe.wait_ge(dec_clear, 1)
            pe.wait_ge(mk_kept, 2)
            pe.wait_ge(keys_in, 32)
            for r in runs:
                r.tensor(pe)
            pe.wait_ge(s.finished, TILES * H)
            empty(bank[0][:, :], k.v[:, 0, :], True)
            with pe.Fori(0, N_B // VR) as i:
                for c in range(VR):
                    pe.wait_ge(pz_ready, i * VR + (N_C + c + 1))
                    pe.wait_ge(v_in[c], i * 16 + 16)
                    nc.tensor.matmul(bank[0][:, :], pz[:, c % 4, :], vg[:, c, :], start=False, stop=False,
                                     skip_group_check=True).then_inc(pz_used, 1)
            empty(bank[0][:, :], k.v[:, 0, :], False).then_inc(closed, 1)

        @block.scalar
        def _(act):
            act.wait_ge(mk_turned, 1)
            for j in range(2):
                nc.scalar.activation(k.mkT[:, 2 * j:2 * j + 2, :].rearrange("p a b -> p (a b)"), bank[j][:, :],
                                     ACT.Copy).then_inc(mk_kept, 1)
            act.wait_ge(pd_max, 1)
            nc.scalar.activation(pd[:], lt[:], ACT.Exp, bias=stat[:, 0:1], accum_out=stat[:, 1:2]).then_inc(pd_exp, 1)
            act.sem_inc(mkd_kept, 2)
            with act.Fori(0, DEC_B // 2) as i:
                for n in range(2 * H):
                    act.wait_ge(mkd_turned, i * 8 + (n + 1))
                    act.wait_ge(mdots, i * 8 + (n + 1))
                    nc.scalar.activation(mkdT[:, n % 2, :], bank[5 + n % 2][:, 0:N_MEM], ACT.Copy).then_inc(mkd_kept, 1)
            act.wait_ge(pm_max, 1)
            nc.scalar.activation(pm[:], bank[4][:, 0:N_MEM], ACT.Exp, bias=stat[:, 4:5], scale=SCALE,
                                 accum_out=stat[:, 5:6]).then_inc(pm_exp, 1)
            act.wait_ge(pm_turned, 1)
            nc.scalar.activation(pmT[:, :, :].rearrange("p a b -> p (a b)"), bank[5][:, 0:2 * P],
                                 ACT.Copy).then_inc(pm_kept, 1)
            act.sem_inc(s.kept_a, 1)
            for r in runs:
                r.scalar(act)
            act.wait_ge(out_in, 32)
            nc.scalar.activation(ed, zd, ACT.Exp, scale=-1.0).then_inc(ed_ready, 1)

        @block.vector
        def _(dve):
            order = Order(dve, order_sem)
            for ap, value in ((ones, 1.0), (zero, 0.0)):
                order(nc.vector.memset(ap[:], value))
            dve.wait_ge(small_in, 16 * (4 + 2 * DEC_T))
            for c in range(2):
                order(nc.vector.scalar_tensor_tensor(
                    lk[:, c, :].rearrange("p (t h) -> p t h", h=H), k.sck[:, c, :].rearrange("p (t h) -> p t h", h=H),
                    SCALE, k.rbias[:].rearrange("p (t c) -> p t c", c=2)[:, :, c:c + 1].to_broadcast([P, NS, H]),
                    ALU.mult, ALU.add))
            order(nc.vector.tensor_tensor(eq[:], k.rids[:].unsqueeze(1).to_broadcast([P, DEC_T, N_B]), nid[:],
                                          ALU.is_equal))
            order(nc.vector.tensor_tensor(nprod[:], kn[:], qr[:].unsqueeze(1).to_broadcast([P, DEC_T, DH]), ALU.mult))
            order.then()
            e2 = eq[:].rearrange("p n (t c) -> p (n t) c", c=2)
            order(nc.vector.tensor_tensor(eqh[:], e2[:, :, 0:1].to_broadcast([P, DEC_T * NS, H]),
                                          e2[:, :, 1:2].to_broadcast([P, DEC_T * NS, H]), ALU.add))
            order(nc.vector.tensor_reduce(nd[:], nprod[:], AX, ALU.add))
            order.then()
            dve.sem_inc(lk_ready, 1)
            dve.wait_ge(lk_turned, 1)
            nbias = nprod[:, 0, 0:DEC_T]
            order(nc.vector.tensor_scalar(nbias, bank[3][:, 0:DEC_T], 1.0, -NEG, ALU.subtract, ALU.mult))
            order(nc.vector.tensor_copy(lt[:, 0:TOPK], bank[2][:, 0:TOPK]))
            order.then()
            order.step(nc.vector.scalar_tensor_tensor(lt[:, TOPK:], nd[:], SCALE, nbias, ALU.mult, ALU.add))
            nc.vector.tensor_reduce(stat[:, 0:1], lt[:], AX, ALU.max, negate=True).then_inc(pd_max, 1)
            dve.wait_ge(pd_exp, 1)
            order.step(nc.vector.reciprocal(stat[:, 2:3], stat[:, 1:2]))
            nc.vector.tensor_scalar(pd[:], pd[:], stat[:, 2:3], None, ALU.mult).then_inc(pd_ready, 1)
            dve.wait_ge(pd_turned, 1)
            order(nc.vector.tensor_copy(pdT[:].rearrange("p a b -> p (a b)"), bank[2][:, 0:2 * P]))
            for i in order.loop(DEC_B // 2, 2 * H):
                for n in range(2 * H):
                    u, h = n // H, n % H
                    dve.wait_ge(mdots, i * 8 + (n + 1))
                    order.step(nc.vector.memset(pz[:, n % 2, :], 0.0))
                    nc.vector.tensor_copy(
                        pz[:, n % 2, :].rearrange("p (b t h) -> p b t h", t=DEC_T, h=H)[:, bass.ds(i * 2 + u, 1), :, h],
                        mqT[:, h, bass.ds(i * 8 + 4 * u, DEC_T)].unsqueeze(1)).then_inc(qz_ready, 1)
            dve.wait_ge(mdots, 3 + DEC_B * H)
            order.step(nc.vector.tensor_reduce(stat[:, 3:4], bank[4][:, 0:N_MEM], AX, ALU.max))
            nc.vector.tensor_scalar(stat[:, 4:5], stat[:, 3:4], -SCALE, None, ALU.mult).then_inc(pm_max, 1)
            dve.wait_ge(pm_exp, 1)
            order.step(nc.vector.reciprocal(stat[:, 6:7], stat[:, 5:6]))
            nc.vector.tensor_scalar(pm[:], pm[:], stat[:, 6:7], None, ALU.mult).then_inc(pm_ready, 1)
            dve.wait_ge(pm_kept, 1)
            for i in order.loop(N_C // 4, 4):
                for c in range(4):
                    dve.wait_ge(pz_used, i * 4 + (c + 1))
                    order.step(nc.vector.memset(pz[:, c, :], 0.0))
                    cols = bass.ds(i * 32 + 16 * (c // 2), 16)
                    nc.vector.tensor_copy(pz[:, c, cols], pmT[:, c % 2, cols]).then_inc(pz_ready, 1)

            def own_head(dst, src):
                order.step(nc.vector.tensor_scalar(dst[:], src[:, 0:DH], hm[:, 0:1], None, ALU.mult))
                for h in range(1, H):
                    order.step(nc.vector.scalar_tensor_tensor(dst[:], src[:, h * DH:(h + 1) * DH], hm[:, h:h + 1],
                                                              dst[:], ALU.mult, ALU.add))

            dve.wait_ge(closed, 1)
            own_head(oc, bank[6])
            dve.sem_inc(out_ready, 1)
            dve.sem_inc(dec_clear, 1)
            for free, slots in ((s.tile_free, 2), (s.read, 2), (s.kept_v, 1), (s.o_free, 2), (s.p_free, 2),
                                (s.mixed, 2), (s.ho_stored[0], 16), (s.ho_stored[1], 16)):
                dve.sem_inc(free, slots)
            for r in runs:
                r.vector(dve, order)
            for i in order.loop(N_B // 4, 4):
                for c in range(4):
                    dve.wait_ge(pz_used, i * 4 + (N_C + c + 1))
                    order.step(nc.vector.memset(pz[:, c, :], 0.0))
                    cols = bass.ds(i * 8 + 4 * (c // 2), 4)
                    nc.vector.tensor_copy(pz[:, c, cols], pdT[:, c % 2, cols]).then_inc(pz_ready, 1)
            dve.wait_ge(closed, 2)
            own_head(ob, bank[0])
            for n in range(DEC_T):
                order.step(nc.vector.scalar_tensor_tensor(ob[:], vn[:, n, :], pd[:, TOPK + n:TOPK + n + 1], ob[:],
                                                          ALU.mult, ALU.add))
            dve.sem_inc(out_ready, 1)
            dve.wait_ge(ed_ready, 1)
            order.step(nc.vector.tensor_scalar(ed, ed, 1.0, None, ALU.add))
            order.step(nc.vector.reciprocal(ed, ed))
            order.step(nc.vector.tensor_tensor(ed, ed, zd, ALU.mult))
            dve.wait_ge(out_in, 48)
            nc.vector.tensor_tensor(od[:], od[:], ed, ALU.mult).then_inc(out_ready, 1)


V1 = ML_D + 1


def mlstm(k):
    nc, ins, outs = k.nc, k.ins, k.outs
    S = k.sem
    consts_in, filled, order_sem = S("mlstm_consts"), S("ones_and_zeros"), S("mlstm_dve_order")
    rows_in, cols_turned, cols_kept = S("gate_rows_loaded"), S("gate_cols_turned"), S("gate_cols_kept")
    loaded, a_stored = k.sems("chunk_loaded", 2), k.sems("a_stored", 2)
    turned, qk_kept, qs_ready = S("qk_turned"), S("qkT_kept"), S("scaled_q_ready")
    s_done, e_ready, dt_ready, sd_ready = S("qk_dots"), S("log_decay"), S("decay_ready"), S("weights_ready")
    kw_ready, kv_done, num_done, c_done = S("weighted_k"), S("kv_done"), S("numerator"), S("state_updated")
    rd_ready, sq_ready, ms_ready, rooted, a_ready = (
        S("inv_denominator"), S("h_squares"), S("h_mean"), S("h_rstd"), S("a_ready"))
    gate_used, zg_ready, gg_ready = S("gate_used"), S("z_gain"), S("output_gate")
    pn_turned, pn_ready, pc_out = S("prompt_n_turned"), S("prompt_n_ready"), S("prompt_state_stored")
    dk_in, d_turned, d_kept, d_pool, d_wide = (
        S("dec_loaded"), S("dec_turned"), S("dec_kept"), S("dec_pool"), S("dec_wide"))
    d_dots, d_dt, d_sd = S("dec_dots"), S("dec_decay"), S("dec_weights")
    st_in, st_stored = k.sems("state_loaded", 4), k.sems("state_stored", 4)
    q_slot, k_slot, d_num, d_kv, d_col, d_c, d_n = (
        S("dec_q_slot"), S("dec_k_slot"), S("dec_num"), S("dec_kv"), S("dec_n_in"), S("dec_state"), S("dec_n_out"))
    d_close, dn_turned, dn_ready, d_out = S("dec_closed"), S("dec_n_turned"), S("dec_n_rows"), S("dec_stored")
    n_in, n_turned, n_kept = S("n_loaded"), S("n_turned"), S("n_kept")
    d_bank_free, wo_in, passed = S("dec_banks_free"), S("w_out_first_loaded"), S("wait_passed")
    K_SCALE = ML_D ** -0.5
    with ExitStack() as st:
        bank = [k.ps(f"mbank_{j}", [P, 512], st) for j in range(8)]
        T = lambda name, shape, dt=F32: k.sb("ml_" + name, shape, dt, at=st)
        rowb = T("rows_everywhere", [P, 2, ML_H, TOK])
        cols = T("cols", [P, NCH + 1, 3, ML_H])
        dkb = T("decay_everywhere", [P, ML_H, 16])
        cmask, gain = T("causal", [P, P]), T("gain", [P, ML_W])
        qin, kin, oin, zin = (T(n, [P, 2, ML_W]) for n in ("q", "k", "o", "z"))
        vin = T("v", [P, 2, ML_H, V1])
        state = T("state", [P, ML_H, 2, V1])
        qkT, qs = T("qkT", [P, 2, 4, P]), T("qs", [P, 2, 2, P])
        ee, dt, sd = (T(n, [P, 2, P]) for n in ("ee", "dt", "sd"))
        kw = T("kw", [P, 2, ML_D])
        gg = T("gg", [P, ML_W])
        a = T("a", [P, 2, ML_W])
        r12 = a[0:3 * ML_H].rearrange("p u n -> p (u n)")[:, 0:TOK]
        small = T("small", [P, 2, 4])
        junk = T("junk", [P, ML_D])
        nrow = T("nrow", [2 * ML_H, P])
        ds = T("dec_states", [P, 4, 2, V1])
        dmask, drow = T("dec_mask", [NS, NS]), T("dec_row_of", [NS, DEC_B])
        dqT, dkT = T("dec_qT", [P, 8, NS]), T("dec_kT", [P, 8, NS])
        dq1, dk1 = T("dec_q_slot", [P, 2, 2, NS]), T("dec_k_slot", [NS, 2, ML_D])
        dkw = T("dec_kw", [NS, ML_W])
        nin, nT, nnT, nout = T("n_in", [NS, ML_D]), T("nT", [P, 2, NS]), T("nnT", [P, 2, NS]), T("n_out", [NS, ML_D])
        zero = T("zero", [P, NS])
        block = st.enter_context(nc.Block())

        @block.sync
        def _(sp):
            sp.dma_start(rowb[:, :, :, :].rearrange("p a h t -> p (a h t)"),
                         k.grows[0:2, :, :].rearrange("(o a) h t -> o (a h t)", o=1).partition_broadcast(P)
                         ).then_inc(rows_in, 16)
            sp.dma_start(r12[:, :], k.grows[2:5, :, :].rearrange("a h t -> (a h) t")).then_inc(rows_in, 16)
            sp.dma_start(dkb[:, :, :].rearrange("p h c -> p (h c)"),
                         k.gdecay[:, :].rearrange("(o h) c -> o (h c)", o=1).partition_broadcast(P)).then_inc(rows_in, 16)
            sp.dma_start(cmask[:, :], ins["causal"][:, :]).then_inc(consts_in, 16)
            sp.dma_start(gain[:, :], ins["g_head"][0:1, :].partition_broadcast(P)).then_inc(consts_in, 16)
            sp.dma_start(dmask[:, :], ins["dec_causal"][:, :]).then_inc(consts_in, 16)
            sp.dma_start(drow[:, :], ins["dec_row_of"][:, :]).then_inc(consts_in, 16)

            def load(rows, r, u, sem):
                for dst, c in ((qin, C_Q), (kin, C_K), (oin, C_O), (zin, C_Z)):
                    sp.dma_start(dst[0:r, u, :], k.proj[rows, c:c + ML_W]).then_inc(sem, 16)
                sp.dma_start(vin[0:r, u, :, 0:ML_D], k.proj[rows, C_V:C_V + ML_W].rearrange("t (h d) -> t h d", h=ML_H)
                             ).then_inc(sem, 16)

            load(slice(0, P), P, 0, loaded[0])
            load(slice(P, 2 * P), P, 1, loaded[1])
            sp.dma_start(k.w_first[:], ins["w_out"][:, 0:O_W].rearrange("(c p) n -> p c n", p=P)).then_inc(wo_in, 16)
            sp.dma_start(nin[:, :], ins["state_mlstm_n"].rearrange("b h d -> (b h) d")).then_inc(n_in, 16)
            for j in range(4):
                sp.dma_start(ds[:, j, :, 0:ML_D], ins["state_mlstm_C"][0, j].rearrange("(c p) v -> p c v", p=P)
                             ).then_inc(st_in[j], 16)

            def store(c, u):
                sp.wait_ge(a_ready, c * ML_H + (2 * ML_H + ML_H))
                sp.dma_start(k.hcat[bass.ds(c * P, P), 0:ML_W], a[:, u, :]).then_inc(a_stored[u], 16)

            with sp.Fori(0, NCH // 2 - 1) as i:
                for u in range(2):
                    store(i * 2 + u, u)
                    load(bass.ds(i * 2 * P + (2 + u) * P, P), P, u, loaded[u])
            for u in range(2):
                store(NCH - 2 + u, u)
                if u == 0:
                    load(slice(SEQ, TOK), NS, 0, dk_in)
            sp.wait_ge(pn_ready, 1)
            for h in range(ML_H):
                sp.dma_start(outs["prompt_C"][h].rearrange("(c p) v -> p c v", p=P), state[:, h, :, 0:ML_D]
                             ).then_inc(pc_out, 16)
            sp.dma_start(outs["prompt_n"].rearrange("h (c p) -> (h c) p", p=P), nrow[:, :]).then_inc(pc_out, 16)
            def state_of(x, b, h):
                return x[bass.ds(b, 1), h].rearrange("o (c p) v -> p (o c) v", p=P)

            with sp.Fori(0, DEC_B - 1) as b:
                for h in range(ML_H):
                    sp.wait_ge(d_n, b * ML_H + (h + 1))
                    sp.dma_start(state_of(outs["sample_C"], b, h), ds[:, h, :, 0:ML_D]).then_inc(st_stored[h], 16)
                for h in range(ML_H):
                    sp.wait_ge(st_stored[h], b * 16 + 16)
                    sp.dma_start(ds[:, h, :, 0:ML_D], state_of(ins["state_mlstm_C"], b + 1, h)).then_inc(st_in[h], 16)
            for h in range(ML_H):
                sp.wait_ge(d_n, (DEC_B - 1) * ML_H + h + 1)
                sp.dma_start(state_of(outs["sample_C"], DEC_B - 1, h), ds[:, h, :, 0:ML_D]).then_inc(st_stored[h], 16)
            sp.wait_ge(dn_ready, 1)
            sp.dma_start(outs["sample_n"].rearrange("b h d -> (b h) d"), nout[:, :]).then_inc(d_out, 16)
            sp.wait_ge(a_ready, 8 + NCH * ML_H + ML_H)
            sp.dma_start(k.hcat[SEQ:TOK, 0:ML_W], a[0:NS, 0, :]).then_inc(d_out, 16)
            sp.wait_ge(d_out, 32)
            sp.wait_ge(wo_in, 16)
            sp.wait_ge(pc_out, 80)
            for j in range(4):
                sp.wait_ge(st_stored[j], 16 * DEC_B)
            for u in range(2):
                sp.wait_ge(a_stored[u], 16 * (NCH // 2 + 1))

        @block.vector
        def _(dve):
            order = Order(dve, order_sem)
            order(nc.vector.memset(state[:], 0.0))
            order(nc.vector.memset(vin[:, :, :, ML_D:], 1.0))
            order(nc.vector.memset(zero[:], 0.0))
            order.then()
            dve.sem_inc(filled, 1)
            for u in range(2):
                dve.sem_inc(a_stored[u], 16)
            dve.sem_inc(a_ready, 2 * ML_H)
            dve.wait_ge(rows_in, 48)
            dve.wait_ge(cols_kept, 2)
            for x in (cols[:, 0:NCH, 2, :], cols[0:NS, NCH, 2, :]):
                nc.vector.tensor_scalar(x, x, K_SCALE, None, ALU.mult).then_inc(cols_kept, 1)
            dve.wait_ge(consts_in, 64)

            def out_gate(r, u, n_g):
                dve.wait_ge(zg_ready, n_g)
                nc.vector.tensor_tensor(gg[0:r], gg[0:r], oin[0:r, u, :], ALU.mult).then_inc(gg_ready, 1)

            def denominator(n, q, r, psum, emn):
                order.step(nc.vector.tensor_scalar(small[0:r, q, 0:1], psum[0:r, ML_D:V1], -1.0, None, ALU.mult))
                order.step(nc.vector.scalar_tensor_tensor(small[0:r, q, 0:1], psum[0:r, ML_D:V1], emn,
                                                          small[0:r, q, 0:1], ALU.max, ALU.max))
                nc.vector.reciprocal(small[0:r, q, 0:1], small[0:r, q, 0:1]).then_inc(rd_ready, 1)

            def output(n, q, r, psum, u, h):
                dve.wait_ge(rooted, n)
                order.step(nc.vector.tensor_tensor(small[0:r, q, 3:4], small[0:r, q, 3:4], small[0:r, q, 0:1], ALU.mult))
                hd = slice(h * ML_D, (h + 1) * ML_D)
                nc.vector.scalar_tensor_tensor(a[0:r, u, hd], psum[0:r, 0:ML_D], small[0:r, q, 3:4], gg[0:r, hd],
                                               ALU.mult, ALU.mult).then_inc(a_ready, 1)

            for i in order.loop(NCH // 2, 16 + 8):

                def scaled_q(j):
                    u, h = j // ML_H, j % ML_H
                    dve.wait_ge(qk_kept, i * 8 + (j + 1))
                    dve.wait_ge(num_done, i * 8 + (j + 1))
                    nc.vector.tensor_tensor(
                        qs[:, j % 2, :, :], qkT[:, j % 2, 0:2, :],
                        rowb[:, 1, h, bass.ds(i * 2 * P + u * P, P)].unsqueeze(1).to_broadcast([P, 2, P]),
                        ALU.mult).then_inc(qs_ready, 1)

                def weights(j):
                    dve.wait_ge(s_done, i * 8 + (j + 3))
                    dve.wait_ge(dt_ready, i * 8 + (j + 3))
                    dve.wait_ge(num_done, i * 8 + (j + 1))
                    nc.vector.scalar_tensor_tensor(
                        sd[:, j % 2, :], bank[2 + 5 * (j % 2)][:, 0:P], K_SCALE, dt[:, j % 2, :],
                        ALU.mult, ALU.mult).then_inc(sd_ready, 1)

                def finish(j):
                    u, h = j // ML_H, j % ML_H
                    if h == 0:
                        dve.wait_ge(a_stored[u], i * 16 + 16)
                        dve.wait_ge(gg_ready, i * 2 + (u + 1))
                    output(i * 8 + (j + 1), j % 2, P, bank[3 + j % 2], u, h)

                scaled_q(0)
                weights(0)
                for j in range(2 * ML_H):
                    u, h, q = j // ML_H, j % ML_H, j % 2
                    if j + 1 < 2 * ML_H:
                        scaled_q(j + 1)
                        weights(j + 1)
                    if j and h == 0:
                        finish(j - 1)
                        dve.wait_ge(a_ready, i * 8 + (j + 8))
                        dve.sem_inc(gate_used, 1)
                    dve.wait_ge(num_done, i * 8 + (j + 3))
                    denominator(j, q, P, bank[3 + q], cols[:, bass.ds(i * 2 + u, 1), 1, h])
                    if h:
                        finish(j - 1)
                    dve.wait_ge(kv_done, i * 8 + (j + 3))
                    dve.wait_ge(c_done, i * 16 + (2 * j + 2))
                    for c in range(2):
                        nc.vector.scalar_tensor_tensor(
                            state[:, h, c, :], state[:, h, c, :], dkb[:, h, bass.ds(i * 2 + u, 1)],
                            bank[5 + c][:, 0:V1], ALU.mult, ALU.add).then_inc(c_done, 1)
                    if h == 0:
                        out_gate(P, u, i * 2 + (u + 1))
                finish(2 * ML_H - 1)
                dve.wait_ge(a_ready, i * 8 + 16)
                dve.sem_inc(gate_used, 1)
            dve.wait_ge(pn_turned, 1)
            nc.vector.tensor_copy(nrow[:, :], bank[7][0:2 * ML_H, 0:P]).then_inc(pn_ready, 1)
            dve.wait_ge(n_turned, 1)
            nc.vector.tensor_copy(nT[:].rearrange("p c n -> p (c n)"), bank[6][:, 0:2 * NS]).then_inc(n_kept, 1)
            dve.wait_ge(d_turned, 1)
            for x, y in ((dqT, 0), (dkT, 1)):
                nc.vector.tensor_copy(x[:].rearrange("p c n -> p (c n)"), bank[y][:, 0:8 * NS]).then_inc(d_kept, 1)
            dve.wait_ge(d_kept, 2)
            dve.wait_ge(d_dots, 1)
            for h in range(ML_H):
                order(nc.vector.tensor_tensor(dqT[:, 2 * h:2 * h + 2, :], dqT[:, 2 * h:2 * h + 2, :],
                                              rowb[:, 1, h, SEQ:TOK].unsqueeze(1).to_broadcast([P, 2, NS]), ALU.mult))
            dve.wait_ge(d_dt, 4)
            for h in range(ML_H):
                order(nc.vector.scalar_tensor_tensor(
                    sd[0:NS, 0, h * NS:(h + 1) * NS], bank[2][0:NS, h * NS:(h + 1) * NS], K_SCALE,
                    dt[0:NS, 0, h * NS:(h + 1) * NS], ALU.mult, ALU.mult))
            order.then()
            dve.sem_inc(d_sd, 1)
            dve.wait_ge(d_pool, 4)
            dve.wait_ge(n_kept, 1)
            with dve.Fori(0, DEC_B) as b:
                for h in range(ML_H):
                    n = b * ML_H + h
                    q = h % 2
                    dve.wait_ge(d_num, n + 1)
                    nc.vector.memset(dq1[:, q, :, :], 0.0).then_inc(d_wide, 1)
                    dve.wait_ge(d_wide, n + 1)
                    cb = bass.ds(b * DEC_T, DEC_T)
                    nc.vector.tensor_copy(dq1[:, q, :, cb], dqT[:, 2 * h:2 * h + 2, cb]).then_inc(q_slot, 1)
                    dve.wait_ge(st_in[h], b * 16 + 16)
                    nc.vector.tensor_copy(ds[:, h, :, ML_D:V1], nT[:, :, bass.ds(b * ML_H + h, 1)]).then_inc(d_col, 1)
                    dve.wait_ge(d_col, n + 1)
                    dve.wait_ge(d_kv, n + 3)
                    dve.wait_ge(d_num, n + 3)
                    for c in range(2):
                        nc.vector.scalar_tensor_tensor(
                            ds[:, h, c, :], ds[:, h, c, :], dkb[:, h, bass.ds(b + 8, 1)],
                            bank[4 + 2 * (h % 2) + c][:, 0:V1], ALU.mult, ALU.add).then_inc(d_c, 1)
                    dve.wait_ge(d_c, n * 2 + 2)
                    dve.sem_inc(d_bank_free, 1)
                    nc.vector.tensor_copy(nnT[:, :, bass.ds(b * ML_H + h, 1)], ds[:, h, :, ML_D:V1]).then_inc(d_n, 1)
            out_gate(NS, 0, NCH + 1)
            dve.wait_ge(gg_ready, NCH + 1)
            dve.wait_ge(d_close, 1)
            dve.wait_ge(a_stored[0], 16 * (NCH // 2 + 1))
            base = NCH * ML_H
            for h in range(ML_H):
                q = h % 2
                if h >= 2:
                    order.then()
                denominator(0, q, NS, bank[h], cols[0:NS, NCH, 1, h:h + 1])
                output(base + h + 1, q, NS, bank[h], 0, h)
                dve.wait_ge(a_ready, 8 + base + h + 1)
            dve.wait_ge(dn_turned, 1)
            nc.vector.tensor_copy(nout[:, :], bank[4][0:NS, 0:ML_D]).then_inc(dn_ready, 1)

        @block.scalar
        def _(act):
            act.wait_ge(cols_turned, 1)
            nc.scalar.activation(cols[:, 0:NCH].rearrange("p c a h -> p (c a h)"), bank[7][:, 0:12 * NCH],
                                 ACT.Copy).then_inc(cols_kept, 1)
            nc.scalar.activation(cols[0:NS, NCH].rearrange("p a h -> p (a h)"), bank[7][0:NS, 12 * NCH:12 * (NCH + 1)],
                                 ACT.Copy).then_inc(cols_kept, 1)
            act.wait_ge(cols_kept, 2)

            with act.Fori(0, NCH // 2) as i:

                def keep(j):
                    act.wait_ge(turned, i * 8 + (j + 1))
                    act.wait_ge(qs_ready, i * 8 + (j + 1))
                    act.wait_ge(s_done, i * 8 + (j + 1))
                    nc.scalar.activation(qkT[:, j % 2, :, :].rearrange("p a b -> p (a b)"), bank[j % 2][:, :],
                                         ACT.Copy).then_inc(qk_kept, 1)
                    act.wait_ge(e_ready, i * 8 + (j + 1))
                    act.wait_ge(sd_ready, i * 8 + (j + 1))
                    u, h = j // ML_H, j % ML_H
                    nc.scalar.activation(dt[:, j % 2, :], ee[:, j % 2, :], ACT.Exp,
                                         bias=cols[:, bass.ds(i * 2 + u, 1), 0, h]).then_inc(dt_ready, 1)

                keep(0)
                keep(1)
                for j in range(2 * ML_H):
                    if j + 2 < 2 * ML_H:
                        keep(j + 2)
                    act.wait_ge(sq_ready, i * 8 + (j + 1))
                    act.wait_ge(rd_ready, i * 8 + (j + 1))
                    nc.scalar.activation(junk[:, :], bank[3 + j % 2][:, 0:ML_D], ACT.Square,
                                         scale=small[:, j % 2, 0:1],
                                         accum_out=small[:, j % 2, 1:2]).then_inc(sq_ready, 1)
            act.wait_ge(e_ready, NCH * ML_H + ML_H)
            act.wait_ge(sd_ready, NCH * ML_H + 2)
            for h in range(ML_H):
                nc.scalar.activation(dt[0:NS, 0, h * NS:(h + 1) * NS], ee[0:NS, 0, h * NS:(h + 1) * NS], ACT.Exp,
                                     bias=cols[0:NS, NCH, 0, h:h + 1]).then_inc(d_dt, 1)
            for h in range(ML_H):
                n = NCH * ML_H + h + 1
                act.wait_ge(sq_ready, n)
                act.wait_ge(rd_ready, n)
                nc.scalar.activation(junk[0:NS, :], bank[h][0:NS, 0:ML_D], ACT.Square, scale=small[0:NS, h % 2, 0:1],
                                     accum_out=small[0:NS, h % 2, 1:2]).then_inc(sq_ready, 1)

        @block.gpsimd
        def _(pool):
            pool.wait_ge(rows_in, 48)
            pool.wait_ge(cols_kept, 4)
            pool.wait_ge(consts_in, 64)

            def root(n, q, r):
                pool.wait_ge(sq_ready, n + 1)
                pool.sem_inc(passed, 1)
                nc.gpsimd.tensor_scalar(small[0:r, q, 2:3], small[0:r, q, 1:2], 1.0 / ML_D, EPS, ALU.mult,
                                        ALU.add).then_inc(ms_ready, 1)
                pool.wait_ge(ms_ready, n)
                nc.gpsimd.tensor_tensor(small[0:r, q, 3:4], small[0:r, q, 2:3], k.mhalf[0:r, :], ALU.pow
                                        ).then_inc(rooted, 1)

            def z_gate(r, u):
                nc.gpsimd.tensor_tensor(gg[0:r], zin[0:r, u, :], gain[0:r], ALU.mult).then_inc(zg_ready, 1)

            with pool.Fori(0, NCH // 2) as i:

                def log_decay(j):
                    u, h, q = j // ML_H, j % ML_H, j % 2
                    pool.wait_ge(dt_ready, i * 8 + (j + 1))
                    nc.gpsimd.tensor_tensor(ee[:, q, :], rowb[:, 0, h, bass.ds(i * 2 * P + u * P, P)], cmask[:],
                                            ALU.add).then_inc(e_ready, 1)

                def weighted(j):
                    u, h, q = j // ML_H, j % ML_H, j % 2
                    if h == 0:
                        pool.wait_ge(loaded[u], i * 80 + 80)
                    pool.wait_ge(kv_done, i * 8 + (j + 1))
                    nc.gpsimd.tensor_tensor(kw[:, q, :], kin[:, u, h * ML_D:(h + 1) * ML_D],
                                            cols[:, bass.ds(i * 2 + u, 1), 2, h].to_broadcast([P, ML_D]),
                                            ALU.mult).then_inc(kw_ready, 1)

                log_decay(0)
                log_decay(1)
                weighted(0)
                for j in range(2 * ML_H):
                    if j + 2 < 2 * ML_H:
                        log_decay(j + 2)
                    if j + 1 < 2 * ML_H:
                        weighted(j + 1)
                    if j % ML_H == 0:
                        u = j // ML_H
                        pool.wait_ge(gate_used, i * 2 + (u + 1))
                        z_gate(P, u)
                    root(i * 8 + (j + 1), j % 2, P)
            pool.wait_ge(dt_ready, NCH * ML_H + 2)
            for h in range(ML_H):
                nc.gpsimd.tensor_tensor(ee[0:NS, 0, h * NS:(h + 1) * NS], rowb[0:NS, 0, h, SEQ:TOK], dmask[:],
                                        ALU.add).then_inc(e_ready, 1)
            pool.wait_ge(dk_in, 80)
            for h in range(ML_H):
                nc.gpsimd.tensor_scalar(dkw[:, h * ML_D:(h + 1) * ML_D], kin[0:NS, 0, h * ML_D:(h + 1) * ML_D],
                                        cols[0:NS, NCH, 2, h:h + 1], None, ALU.mult).then_inc(d_pool, 1)
            pool.wait_ge(gate_used, NCH + 1)
            z_gate(NS, 0)
            pool.wait_ge(d_pool, 4)
            with pool.Fori(0, DEC_B) as b:
                for h in range(ML_H):
                    pool.wait_ge(d_kv, b * ML_H + (h + 1))
                    pool.sem_inc(passed, 1)
                    nc.gpsimd.tensor_tensor(dk1[:, h % 2, :], dkw[:, h * ML_D:(h + 1) * ML_D],
                                            drow[:, bass.ds(b, 1)].to_broadcast([NS, ML_D]), ALU.mult
                                            ).then_inc(k_slot, 1)
            for h in range(ML_H):
                root(NCH * ML_H + h + 1, h % 2, NS)

        @block.tensor
        def _(pe):
            for sem, v in ((num_done, 2), (s_done, 2), (sd_ready, 2), (sq_ready, 1), (gate_used, 1),
                           (kv_done, 2), (dt_ready, 2), (c_done, 2), (qs_ready, 2)):
                pe.sem_inc(sem, v)
            pe.wait_ge(filled, 1)
            pe.wait_ge(rows_in, 48)
            for c in range(NCH + 1):
                w = P if c < NCH else NS
                last = nc.tensor.transpose(bank[7][0:w, 12 * c:12 * c + 12], r12[:, c * P:c * P + w],
                                           k.ident[0:12, 0:12])
            last.then_inc(cols_turned, 1)
            with pe.Fori(0, NCH // 2) as i:

                def turn(j):
                    u, h = j // ML_H, j % ML_H
                    if h == 0:
                        pe.wait_ge(loaded[u], i * 80 + 80)
                    for c in range(2):
                        for x, at in ((qin, 0), (kin, 2)):
                            last = nc.tensor.transpose(bank[j % 2][:, (at + c) * P:(at + c + 1) * P],
                                                       x[:, u, h * ML_D + c * P:h * ML_D + (c + 1) * P], k.ident[:])
                    last.then_inc(turned, 1)

                def dots(j):
                    pe.wait_ge(qk_kept, i * 8 + (j + 1))
                    pe.wait_ge(sd_ready, i * 8 + (j + 1))
                    for c in range(2):
                        last = nc.tensor.matmul(bank[2 + 5 * (j % 2)][:, 0:P], qkT[:, j % 2, 2 + c, :],
                                                qkT[:, j % 2, c, :], start=c == 0, stop=c == 1)
                    last.then_inc(s_done, 1)

                turn(0)
                dots(0)
                turn(1)
                for j in range(2 * ML_H):
                    u, h, q = j // ML_H, j % ML_H, j % 2
                    if j + 1 < 2 * ML_H:
                        dots(j + 1)
                    pe.wait_ge(sd_ready, i * 8 + (j + 3))
                    pe.wait_ge(qs_ready, i * 8 + (j + 3))
                    pe.wait_ge(a_ready, i * 8 + (j + 1 + 2 * ML_H - 2))
                    nc.tensor.matmul(bank[3 + q][:, 0:V1], sd[:, q, :], vin[:, u, h, :], start=True, stop=False)
                    for c in range(2):
                        last = nc.tensor.matmul(bank[3 + q][:, 0:V1], qs[:, q, c, :], state[:, h, c, :],
                                                start=False, stop=c == 1)
                    last.then_inc(num_done, 1)
                    if j + 2 < 2 * ML_H:
                        turn(j + 2)
                    pe.wait_ge(kw_ready, i * 8 + (j + 1))
                    pe.wait_ge(c_done, i * 16 + (2 * j + 2))
                    for c in range(2):
                        last = nc.tensor.matmul(bank[5 + c][:, 0:V1], kw[:, q, c * P:(c + 1) * P], vin[:, u, h, :],
                                                start=True, stop=True)
                    last.then_inc(kv_done, 1)
            pe.wait_ge(c_done, 2 + 2 * NCH * ML_H)
            nc.tensor.transpose(bank[7][0:2 * ML_H, 0:P], state[:, :, :, ML_D].rearrange("p h c -> p (h c)"),
                                k.ident[:]).then_inc(pn_turned, 1)
            pe.wait_ge(n_in, 16)
            for c in range(2):
                last = nc.tensor.transpose(bank[6][:, c * NS:(c + 1) * NS], nin[:, c * P:(c + 1) * P],
                                           k.ident[0:NS, 0:NS])
            last.then_inc(n_turned, 1)
            pe.wait_ge(dk_in, 80)
            for x, y in ((qin, 0), (kin, 1)):
                for c in range(8):
                    last = nc.tensor.transpose(bank[y][:, c * NS:(c + 1) * NS], x[0:NS, 0, c * P:(c + 1) * P],
                                               k.ident[0:NS, 0:NS])
            last.then_inc(d_turned, 1)
            pe.wait_ge(d_kept, 2)
            for h in range(ML_H):
                for c in range(2):
                    last = nc.tensor.matmul(bank[2][0:NS, h * NS:(h + 1) * NS], dkT[:, 2 * h + c, :],
                                            dqT[:, 2 * h + c, :], start=c == 0, stop=c == 1)
            last.then_inc(d_dots, 1)
            pe.wait_ge(d_sd, 1)
            pe.wait_ge(n_kept, 1)
            pe.wait_ge(pn_ready, 1)
            pe.wait_ge(a_ready, 8 + NCH * ML_H)
            for h in range(ML_H):
                nc.tensor.matmul(bank[h][0:NS, 0:V1], sd[0:NS, 0, h * NS:(h + 1) * NS], vin[0:NS, 0, h, :],
                                 start=True, stop=False, skip_group_check=True)
            pe.sem_inc(d_num, 2)
            pe.sem_inc(d_kv, 2)
            pe.sem_inc(d_bank_free, 2)
            with pe.Fori(0, DEC_B) as b:
                for h in range(ML_H):
                    n = b * ML_H + h
                    q = h % 2
                    pe.wait_ge(k_slot, n + 1)
                    pe.wait_ge(d_bank_free, n + 1)
                    for c in range(2):
                        last = nc.tensor.matmul(bank[4 + 2 * q + c][:, 0:V1], dk1[:, q, c * P:(c + 1) * P],
                                                vin[0:NS, 0, h, :], start=True, stop=True)
                    last.then_inc(d_kv, 1)
                    pe.wait_ge(q_slot, n + 1)
                    pe.wait_ge(d_col, n + 1)
                    for c in range(2):
                        last = nc.tensor.matmul(bank[h][0:NS, 0:V1], dq1[:, q, c, :], ds[:, h, c, :], start=False,
                                                stop=False, skip_group_check=True)
                    last.then_inc(d_num, 1)
            for h in range(ML_H):
                last = nc.tensor.matmul(bank[h][0:NS, 0:V1], zero[0:NS, :], vin[0:NS, 0, h, :], start=False, stop=True,
                                        skip_group_check=True)
            last.then_inc(d_close, 1)
            pe.wait_ge(d_n, NS)
            for c in range(2):
                last = nc.tensor.transpose(bank[4][0:NS, c * P:(c + 1) * P], nnT[:, c, :], k.ident[:])
            last.then_inc(dn_turned, 1)




O_W = 512
O_B = D // O_W


def project_out(k):
    nc, ins, outs = k.nc, k.ins, k.outs
    S = k.sem
    w_in_, g_in, h_in, y_out = k.sems("w_out_loaded", O_B), S("g_post_loaded"), k.sems("h_x_loaded", 2), k.sems("y_stored", 2)
    turned, hT_a, hT_v, done, used = S("h_turned"), S("hT_by_act"), S("hT_by_dve"), S("out_bank_ready"), S("hT_used")
    scaled, squared, meaned, rooted, y_ready = (
        S("out_scaled"), S("out_squared"), S("out_mean"), S("out_rstd"), S("y_ready"))
    order_sem = S("out_dve_order")
    with ExitStack() as st:
        turn = [k.ps(f"oturn{j}", [P, 4, P], st) for j in range(4)]
        acc = [k.ps(f"oacc{j}", [P, O_W], st) for j in range(O_B)]
        w = k.sb("w_out_sb", [P, KT, D - O_W], at=st)
        hin, xin = k.sb("h_sb", [P, 2, D], at=st), k.sb("x_sb", [P, 2, D], at=st)
        hT, y = k.sb("hT", [P, 2, KT, P], at=st), k.sb("y_sb", [P, 2, D], at=st)
        g, junk = k.sb("g_post_sb", [P, D], at=st), k.sb("ojunk", [P, O_W], at=st)
        ss, ms = k.sb("oss", [P, 2, O_B], at=st), k.sb("oms", [P, 2, 2], at=st)
        block = st.enter_context(nc.Block())

        def rows(n):
            if isinstance(n, int) and n == QT:
                return NS, slice(SEQ, TOK), ins["x_sample"][:, :], outs["y_sample"][:, :]
            at = bass.ds(n * P, P)
            return P, at, ins["x_prompt"][at, :], outs["y_prompt"][at, :]

        def tiles(eng, order=None, per=0):
            rounds = order.loop(QT // 2 - 1, per) if order else None
            if rounds is None:
                with eng.Fori(0, QT // 2 - 1) as i:
                    for u in range(2):
                        yield i * 2 + u, u, P
            else:
                for i in rounds:
                    for u in range(2):
                        yield i * 2 + u, u, P
            for n in range(QT - 2, QT + 1):
                yield n, n % 2, P if n < QT else NS

        def after(n):
            return {QT: 0, QT - 1: NS}.get(n, P) if isinstance(n, int) else P

        @block.sync
        def _(sp):
            def load(n, u):
                r, at, x, _ = rows(n)
                sp.dma_start(hin[0:r, u, :], k.hcat[at, :]).then_inc(h_in[u], 16)
                sp.dma_start(xin[0:r, u, :], x).then_inc(h_in[u], 16)

            load(0, 0)
            sp.dma_start(g[:], ins["g_post"][0:1, :].partition_broadcast(P)).then_inc(g_in, 16)
            for b in range(1, O_B):
                sp.dma_start(w[:, :, (b - 1) * O_W:b * O_W],
                             ins["w_out"][:, b * O_W:(b + 1) * O_W].rearrange("(c p) n -> p c n", p=P)
                             ).then_inc(w_in_[b], 16)
                if b == 1:
                    load(1, 1)
            for n, u, r in tiles(sp):
                sp.wait_ge(y_ready, n + 1)
                sp.dma_start(rows(n)[3], y[0:r, u, :]).then_inc(y_out[u], 16)
                if not (isinstance(n, int) and n > QT - 2):
                    load(n + 2, u)
            sp.wait_ge(y_out[0], 16 * (QT // 2 + 2))
            sp.wait_ge(y_out[1], 16 * (QT // 2 + 1))

        @block.scalar
        def _(act):
            def keep(m, u, r):
                act.wait_ge(turned, m + 1)
                act.wait_ge(used, m + 1)
                for b in range(2):
                    nc.scalar.activation(hT[:, u, 4 * b:4 * b + 4, 0:r], turn[b][:, :, 0:r], ACT.Copy
                                         ).then_inc(hT_a, 1)

            keep(0, 0, P)
            for n, u, r in tiles(act):
                for b in range(O_B):
                    act.wait_ge(scaled, n * O_B + (b + 1))
                    act.wait_ge(meaned, n + 1)
                    act.wait_ge(squared, n * O_B + (b + 1 + O_B))
                    nc.scalar.activation(junk[0:r, :], acc[b][0:r, :], ACT.Square,
                                         accum_out=ss[0:r, u, b:b + 1]).then_inc(squared, 1)
                    if b == 0 and after(n):
                        keep(n + 1, 1 - u, after(n))

        @block.gpsimd
        def _(pool):
            for n, u, r in tiles(pool):
                pool.wait_ge(meaned, n + 3)
                nc.gpsimd.tensor_tensor(ms[0:r, u, 1:2], ms[0:r, u, 0:1], k.mhalf[0:r, :], ALU.pow
                                        ).then_inc(rooted, 1)

        @block.vector
        def _(dve):
            order = Order(dve, order_sem)
            for u in range(2):
                dve.sem_inc(y_out[u], 16)

            def keep(m, u, r):
                dve.wait_ge(turned, m + 1)
                dve.wait_ge(used, m + 1)
                for b in range(2, 4):
                    nc.vector.tensor_copy(hT[:, u, 4 * b:4 * b + 4, 0:r], turn[b][:, :, 0:r]).then_inc(hT_v, 1)

            keep(0, 0, P)
            dve.wait_ge(g_in, 16)
            for n, u, r in tiles(dve, order, 2):
                dve.wait_ge(y_out[u], (n - u) * 8 + 16 if not isinstance(n, int) else n // 2 * 16 + 16)
                for b in range(O_B):
                    dve.wait_ge(done, n * O_B + (b + 1))
                    cols = slice(b * O_W, (b + 1) * O_W)
                    nc.vector.tensor_tensor(y[0:r, u, cols], acc[b][0:r, :], g[0:r, cols], ALU.mult
                                            ).then_inc(scaled, 1)
                    if b == 0 and after(n):
                        keep(n + 1, 1 - u, after(n))
                dve.wait_ge(squared, n * O_B + (2 * O_B + 1))
                order.step(nc.vector.tensor_reduce(ms[0:r, u, 0:1], ss[0:r, u, :], AX, ALU.add))
                nc.vector.tensor_scalar(ms[0:r, u, 0:1], ms[0:r, u, 0:1], 1.0 / D, EPS, ALU.mult, ALU.add
                                        ).then_inc(meaned, 1)
                dve.wait_ge(rooted, n + 1)
                dve.wait_ge(scaled, n * O_B + O_B)
                dve.wait_ge(h_in[u], (n - u) * 16 + 32 if not isinstance(n, int) else n // 2 * 32 + 32)
                nc.vector.scalar_tensor_tensor(y[0:r, u, :], y[0:r, u, :], ms[0:r, u, 1:2], xin[0:r, u, :], ALU.mult,
                                               ALU.add).then_inc(y_ready, 1)

        @block.tensor
        def _(pe):
            pe.sem_inc(used, 2)
            pe.sem_inc(meaned, 2)
            pe.sem_inc(squared, 1 + O_B)

            def turning(m, u, r):
                pe.wait_ge(h_in[u], (m - u) * 16 + 32 if not isinstance(m, int) else m // 2 * 32 + 32)
                if not (isinstance(m, int) and m == 0):
                    pe.wait_ge(hT_a, m * 2)
                    pe.wait_ge(hT_v, m * 2)
                for c in range(KT):
                    last = nc.tensor.transpose(turn[c // 4][:, c % 4, 0:r], hin[0:r, u, c * P:(c + 1) * P],
                                               k.ident[0:r, 0:r])
                last.then_inc(turned, 1)

            turning(0, 0, P)
            for n, u, r in tiles(pe):
                pe.wait_ge(hT_a, n * 2 + 2)
                pe.wait_ge(hT_v, n * 2 + 2)
                for b in range(O_B):
                    if b:
                        pe.wait_ge(w_in_[b], 16)
                    pe.wait_ge(squared, n * O_B + (b + 2))
                    for c in range(KT):
                        wb = k.w_first[:, c, :] if b == 0 else w[:, c, (b - 1) * O_W:b * O_W]
                        last = nc.tensor.matmul(acc[b][0:r, :], hT[:, u, c, 0:r], wb, start=c == 0, stop=c == KT - 1)
                    last.then_inc(done, 1)
                    if b == 0 and after(n):
                        turning(n + 1, 1 - u, after(n))
                pe.wait_ge(done, n * O_B + O_B)
                pe.sem_inc(used, 1)


def build(nc, ins, outs):
    k = Program(nc, ins, outs)
    with k.outer, nc.allow_non_contiguous_dma("small tables change layout on their way"):
        k.w_in_v = ins["w_in"].rearrange("(c p) n -> p c n", p=P)
        k.proj = k.scratch("proj", [TOK, IN_W])
        k.headT = k.scratch("headT", [P, T_SLOTS, TOK])
        k.ident = k.sb("ident_sb", [P, P])
        k.mhalf = k.sb("mhalf", [P, 1])
        k.sq = k.scratch("roped_q_of_decode", [NS, HW])
        k.iws = k.scratch("decode_index_weights", [DEC_B, IDX_H, DEC_T])
        k.pt4 = k.scratch("pages_of_token", [DEC_B, DEC_T, N_PAGES], I32)
        k.cand = k.scratch("candidates", [NS, 4, TOPK], I32)
        k.rid_d = k.scratch("row_ids", [P, S_COLS], I32)
        k.adr = k.scratch("selected_candidates", [NS * TOPK], I32)
        k.sel = k.scratch("selection_bias", [SEQ, SEQ])
        k.kn4 = k.scratch("new_keys_of_rows", [DEC_T, DEC_B, DEC_T, HW])
        k.vn4 = k.scratch("new_values_of_rows", [DEC_T, DEC_B, DEC_T, HW])
        k.odec = k.scratch("decode_attention", [2, NS, HW])
        k.hcat = k.scratch("hcat", [TOK, D])
        k.grows = k.scratch("gate_rows", [5, ML_H, TOK])
        k.gdecay = k.scratch("gate_decay", [ML_H, 16])
        k.rids = k.sb("rids", [P, 2 * NS], I32)
        k.rowid = k.sb("rowid", [P, 2 * NS], I32)
        k.rbias = k.sb("rbias", [P, 2 * NS])
        k.sck = k.sb("key_dots", [P, 2, P])
        with ExitStack() as xs:
            k.xT = k.sb("xT", [P, KT, TOK], at=xs)
            with ExitStack() as ms:
                k.memT = k.sb("memT", [P, KT, N_MEM], at=ms)
                k.run(normalise)
                k.run(project_first)
            k.run(rotate)
            k.run(select)
        k.run(attend)
        k.w_first = k.sb("w_out_first", [P, KT, O_W])
        k.run(mlstm)
        k.run(project_out)


def tables():
    pos = np.concatenate([np.arange(SEQ), np.tile(PAST + np.arange(DEC_T), DEC_B)]).astype(np.float32)

    def rot(half):
        inv = (10000.0 ** (-np.arange(half) / half)).astype(np.float32)
        ang = pos[:, None] * inv[None, :]
        return np.stack([np.cos(ang), np.sin(ang)], 1).astype(np.float32)

    row = np.arange(P)
    g, b, t = row // NS, row % NS // DEC_T, row % DEC_T
    new = np.arange(DEC_T)
    new_bias = np.where((g[:, None] == 0) & (new[None] <= t[:, None]), 0.0, NEG)
    db, ds_, dt_ = row // 64, row // 32 % 2, row % DEC_T
    pick = np.zeros((P, 2, 2, DEC_T))
    pick[row, ds_, db, dt_] = IDX_SCALE
    tok = np.arange(TOK)
    chunk_start = np.where(tok < SEQ, tok % CHUNK == 0, tok % DEC_T == 0)
    s_, t_ = np.arange(NS)[:, None], np.arange(NS)[None]
    return {
        "not_first": (1.0 - chunk_start).astype(np.float32)[None],
        "dec_first": np.where((tok >= SEQ) & chunk_start, -1e30, 0.0).astype(np.float32)[None],
        "causal": np.where(row[:, None] <= row[None], 0.0, -1e30).astype(np.float32),
        "dec_causal": np.where((s_ // DEC_T == t_ // DEC_T) & (s_ <= t_), 0.0, -1e30).astype(np.float32),
        "dec_row_of": (np.arange(NS)[:, None] // DEC_T == np.arange(DEC_B)[None]).astype(np.float32),
        "rot128": rot(DH // 2), "rot64": rot(IDX_D // 2), "ident": np.eye(P, dtype=np.float32),
        "kpos": np.arange(512, dtype=np.float32)[None],
        "qrel": (row[:, None] + np.array([[i * P - 512 * f for i in range(QT) for f in range(2)]])).astype(np.float32),
        "new_bias": new_bias.astype(np.float32), "pick": pick.reshape(P, 16).astype(np.float32),
        "slot0": (2 * 32 * (g // 2) + g % 2).astype(np.float32)[:, None],
        "slot_step": (2 * np.arange(32, dtype=np.float32))[None],
        "new_ids": np.repeat((N_POOL * PAGE + np.arange(DEC_B)[None] * DEC_T + new[:, None])[:, :, None],
                             2 * DEC_T, 2).reshape(1, -1).astype(np.float32),
        "head_pick": (row[:, None] % H == np.arange(H)[None]).astype(np.float32),
        "new_rid": (N_POOL * PAGE + b[:, None] * DEC_T + new[None]).astype(np.int32),
        "row_base": (row * S_COLS).astype(np.float32)[:, None],
        "cand_base": (np.arange(NS) * 4 * TOPK).astype(np.float32)[:, None],
    }


VIEWS = {
    "x_prompt": (SEQ, D), "x_sample": (NS, D), "state_mlstm_C": (DEC_B, ML_H, ML_D, ML_D),
    "state_mlstm_n": (DEC_B, ML_H, ML_D), "state_mlstm_m": (DEC_B, ML_H),
    "cache_k": (N_POOL * PAGE, HW), "cache_v": (N_POOL * PAGE, HW), "cache_kidx": (N_POOL, PAGE * IDX_D),
    "cache_mem_k": (DEC_B, N_MEM, HW), "cache_mem_v": (DEC_B, N_MEM, HW), "page_table": (DEC_B, N_PAGES),
    "mem_prompt": (N_MEM, D), "g_pre": (1, D), "w_in": (D, IN_W), "b_gates": (1, 2 * ML_H),
    "g_head": (1, ML_W), "w_mem_k": (D, HW), "w_mem_v": (D, HW), "g_mem": (1, D), "w_out": (D, D),
    "g_post": (1, D),
}
OUTS = {
    "y_prompt": ((SEQ, D), (1, SEQ, D)), "y_sample": ((NS, D), (DEC_B, DEC_T, D)),
    "prompt_C": ((ML_H, ML_D, ML_D), (1, 1, ML_H, ML_D, ML_D)),
    "prompt_n": ((ML_H, ML_D), (1, 1, ML_H, ML_D)), "prompt_m": ((ML_H, 1), (1, 1, ML_H)),
    "prompt_k": ((SEQ, HW), (1, 1, SEQ, H, DH)), "prompt_v": ((SEQ, HW), (1, 1, SEQ, H, DH)),
    "prompt_kidx": ((SEQ, IDX_D), (1, 1, SEQ, IDX_D)),
    "prompt_mem_k": ((N_MEM, HW), (1, 1, N_MEM, H, DH)), "prompt_mem_v": ((N_MEM, HW), (1, 1, N_MEM, H, DH)),
    "sample_C": ((DEC_B, ML_H, ML_D, ML_D), (1, DEC_B, ML_H, ML_D, ML_D)),
    "sample_n": ((DEC_B, ML_H, ML_D), (1, DEC_B, ML_H, ML_D)), "sample_m": ((DEC_B, ML_H), (1, DEC_B, ML_H)),
    "sample_k": ((NS, HW), (1, DEC_B, DEC_T, H, DH)), "sample_v": ((NS, HW), (1, DEC_B, DEC_T, H, DH)),
    "sample_kidx": ((NS, IDX_D), (1, DEC_B, DEC_T, IDX_D)),
}


def kernel(**inputs):
    import concourse.bacc as bacc
    from concourse.bass_utils import run_bass_kernel_spmd

    nc = bacc.Bacc("TRN2", target_bir_lowering=False, num_devices=1)
    arrays = {name: np.ascontiguousarray(inputs[name]).reshape(shape) for name, shape in VIEWS.items()}
    arrays.update(tables())
    ins = {n: nc.dram_tensor(f"in_{n}", a.shape, mybir.dt.from_np(a.dtype), kind="ExternalInput").ap()
           for n, a in arrays.items()}
    outs = {n: nc.dram_tensor(f"out_{n}", s, F32, kind="ExternalOutput").ap() for n, (s, _) in OUTS.items()}
    build(nc, ins, outs)
    r = run_bass_kernel_spmd(nc, [{f"in_{n}": a for n, a in arrays.items()}], core_ids=[0])
    return tuple(r.results[0][f"out_{n}"].reshape(full) for n, (_, full) in OUTS.items())
```
